# Optimizing a Trainium2 kernel written in Bass

```python
import math
import jax, jax.numpy as jnp
from jax import lax
import numpy as np

D_MODEL = 1024
BATCH = 1
SEQ = 256
DEPTH = 2

CHUNK = 64
Q_BLOCK = 128
NORM_EPS = 1e-6
DA_HEADS = 4
DA_DK = 64
DA_DV = 2 * DA_DK
HG_HEADS = 4
HG_DK = 128
HG_DV = 128
ML_HEADS = 4
ML_DK = 128
ML_DV = 128
ML_CONV = 4
N_BRANCH = 3
BRANCH_W = 512
D_FF = 2816
N_EXPERTS = 8
TOP_K = 2
N_DENSE = (DEPTH + 1) // 2
N_MOE = DEPTH // 2

A_QK = DA_HEADS * DA_DK
COLS = (('a_q1', A_QK), ('a_q2', A_QK), ('a_k1', A_QK), ('a_k2', A_QK),
        ('a_v', DA_HEADS * DA_DV),
        ('b_q', HG_HEADS * HG_DK), ('b_f', HG_HEADS * HG_DK),
        ('b_i', HG_HEADS * HG_DV), ('b_g', HG_HEADS * HG_DV),
        ('c_qk', 2 * ML_HEADS * ML_DK), ('c_v', ML_HEADS * ML_DV),
        ('c_o', ML_HEADS * ML_DV), ('c_i', ML_HEADS), ('c_f', ML_HEADS),
        ('gate', N_BRANCH * D_MODEL))
COL_NAMES = tuple(n for n, _ in COLS)
COL_OFFSETS = tuple(int(v) for v in np.cumsum([s for _, s in COLS])[:-1])
D_IN = sum(s for _, s in COLS)


def _rmsnorm(x, w):
    xf = x.astype(jnp.float32)
    y = xf * lax.rsqrt(jnp.mean(xf * xf, axis=-1, keepdims=True) + NORM_EPS)
    return (y * w.astype(jnp.float32)).astype(x.dtype)

def _modulate(xn, shift, scale):
    return xn * (1.0 + scale[:, None, :]) + shift[:, None, :]

def _swiglu(h, w1, w3, w2):
    return (jax.nn.silu(h @ w1) * (h @ w3)) @ w2

def _causal_conv(u, w, b):
    K = w.shape[0]
    S = u.shape[1]
    up = jnp.pad(u, ((0, 0), (K - 1, 0), (0, 0)))
    y = up[:, 0:S] * w[0] + b
    for j in range(1, K):
        y = y + up[:, j:j + S] * w[j]
    return y

def _diff_attention(q1, q2, k1, k2, v, lam, lam_init, qn_w, kn_w, subln_w):
    B, S, H, dk = q1.shape
    dv = v.shape[-1]
    f32 = jnp.float32
    q = _rmsnorm(jnp.stack([q1, q2], axis=2).astype(f32), qn_w) * (dk ** -0.5)
    k = _rmsnorm(jnp.stack([k1, k2], axis=2).astype(f32), kn_w)
    q = q.transpose(0, 3, 2, 1, 4)
    k = k.transpose(0, 3, 2, 1, 4)
    vf = v.astype(f32).transpose(0, 2, 1, 3)
    slopes = jnp.asarray(2.0 ** (-8.0 * np.arange(1, H + 1) / H), dtype=f32)
    kpos = jnp.arange(S)
    kchunk = kpos // CHUNK

    def block(j):
        start = j * Q_BLOCK
        qb = lax.dynamic_slice_in_dim(q, start, Q_BLOCK, axis=3)
        qpos = start + jnp.arange(Q_BLOCK)
        s = jnp.einsum('bhmqd,bhmkd->bhmqk', qb, k)
        dist = jnp.abs(qpos[:, None] - kpos[None, :]).astype(f32)
        mask = kchunk[None, :] <= (qpos // CHUNK)[:, None]
        s = jnp.where(mask, s - (slopes[:, None, None] * dist)[None, :, None], -jnp.inf)
        p = jax.nn.softmax(s, axis=-1)
        a = p[:, :, 0] - lam * p[:, :, 1]
        return jnp.einsum('bhqk,bhkd->bhqd', a, vf)

    o = lax.map(block, jnp.arange(S // Q_BLOCK))
    o = o.transpose(1, 0, 3, 2, 4).reshape(B, S, H, dv)
    o = _rmsnorm(o, subln_w) * (1.0 - lam_init)
    return o.reshape(B, S, H * dv).astype(v.dtype)

def _hgrn2(q, f_pre, i, g, lb, gnorm_w):
    B, S, H, dk = q.shape
    dv = i.shape[-1]
    n = S // CHUNK
    f32 = jnp.float32
    qf = jax.nn.silu(q.astype(f32))
    lb = lb.astype(f32).reshape(H, dk)
    logf = jnp.logaddexp(jnp.log(lb), jnp.log1p(-lb) + jax.nn.log_sigmoid(f_pre.astype(f32)))
    kf = -jnp.expm1(logf)
    vf = i.astype(f32)

    def to_chunks(t):
        return t.reshape(B, n, CHUNK, H, t.shape[-1]).transpose(1, 0, 3, 2, 4)

    causal = jnp.tril(jnp.ones((CHUNK, CHUNK), dtype=bool))

    def step(state, inp):
        qc, kc, vc, lfc = inp
        b = jnp.cumsum(lfc, axis=2)
        o_inter = jnp.einsum('bhtd,bhde->bhte', qc * jnp.exp(b), state)
        diff = b[:, :, :, None, :] - b[:, :, None, :, :]
        dec = jnp.exp(jnp.where(causal[:, :, None], diff, -jnp.inf))
        att = jnp.einsum('bhtd,bhsd,bhtsd->bhts', qc, kc, dec)
        o_intra = jnp.einsum('bhts,bhse->bhte', att, vc)
        b_last = b[:, :, -1:, :]
        state = (jnp.exp(b_last[:, :, 0, :])[..., None] * state
                 + jnp.einsum('bhsd,bhse->bhde', kc * jnp.exp(b_last - b), vc))
        return state, o_inter + o_intra

    s0 = jnp.zeros((B, H, dk, dv), f32)
    _, o = lax.scan(step, s0, (to_chunks(qf), to_chunks(kf), to_chunks(vf), to_chunks(logf)))
    o = o.transpose(1, 0, 3, 2, 4).reshape(B, S, H, dv)
    o = _rmsnorm(o, gnorm_w) * jax.nn.silu(g.astype(f32))
    return o.reshape(B, S, H * dv).astype(g.dtype)

def _mlstm(q, k, v, o_pre, i_pre, f_pre, norm_w):
    B, S, H, dk = q.shape
    dv = v.shape[-1]
    n = S // CHUNK
    f32 = jnp.float32
    qf = q.astype(f32)
    kf = k.astype(f32) * (dk ** -0.5)
    vf = v.astype(f32)
    ig = i_pre.astype(f32)
    lf = jax.nn.log_sigmoid(f_pre.astype(f32))

    def to_chunks(t):
        return t.reshape(B, n, CHUNK, H, t.shape[-1]).transpose(1, 0, 3, 2, 4)

    def gate_chunks(t):
        return t.reshape(B, n, CHUNK, H).transpose(1, 0, 3, 2)

    causal = jnp.tril(jnp.ones((CHUNK, CHUNK), dtype=bool))

    def step(carry, inp):
        C, nv, m = carry
        qc, kc, vc, igc, lfc = inp
        b = jnp.cumsum(lfc, axis=-1)
        log_d = jnp.where(causal, b[..., :, None] - b[..., None, :] + igc[..., None, :], -jnp.inf)
        log_inter = b + m[..., None]
        m_t = jnp.maximum(log_inter, jnp.max(log_d, axis=-1))
        w_intra = jnp.exp(log_d - m_t[..., None]) * jnp.einsum('bhtd,bhsd->bhts', qc, kc)
        w_inter = jnp.exp(log_inter - m_t)
        num = (w_inter[..., None] * jnp.einsum('bhtd,bhde->bhte', qc, C)
               + jnp.einsum('bhts,bhse->bhte', w_intra, vc))
        dot = w_inter * jnp.einsum('bhtd,bhd->bht', qc, nv) + jnp.sum(w_intra, axis=-1)
        h = num / jnp.maximum(jnp.abs(dot), jnp.exp(-m_t))[..., None]
        g = b[..., -1]
        log_w = g[..., None] - b + igc
        m_new = jnp.maximum(g + m, jnp.max(log_w, axis=-1))
        w_s = jnp.exp(log_w - m_new[..., None])
        decay = jnp.exp(g + m - m_new)
        C = decay[..., None, None] * C + jnp.einsum('bhs,bhsd,bhse->bhde', w_s, kc, vc)
        nv = decay[..., None] * nv + jnp.einsum('bhs,bhsd->bhd', w_s, kc)
        return (C, nv, m_new), h

    init = (jnp.zeros((B, H, dk, dv), f32), jnp.zeros((B, H, dk), f32), jnp.zeros((B, H), f32))
    _, h = lax.scan(step, init, (to_chunks(qf), to_chunks(kf), to_chunks(vf),
                                 gate_chunks(ig), gate_chunks(lf)))
    h = h.transpose(1, 0, 3, 2, 4).reshape(B, S, H, dv)
    h = _rmsnorm(h, norm_w) * jax.nn.sigmoid(o_pre.astype(f32))
    return h.reshape(B, S, H * dv).astype(v.dtype)

def _mixer(h, w_in, conv_w, conv_b, qn_w, kn_w, lq1, lk1, lq2, lk2, subln_w, lam_init,
           lb, gnorm_w, ib, fb, cnorm_w, w_branch, w_out):
    B, S, _ = h.shape
    f32 = jnp.float32
    parts = dict(zip(COL_NAMES, jnp.split(w_in, COL_OFFSETS, axis=1)))

    def proj(name):
        return h @ parts[name]

    def heads(t, nh):
        return t.reshape(B, S, nh, -1)

    lam = (jnp.exp(jnp.sum(lq1.astype(f32) * lk1.astype(f32)))
           - jnp.exp(jnp.sum(lq2.astype(f32) * lk2.astype(f32))) + lam_init)
    y_a = _diff_attention(heads(proj('a_q1'), DA_HEADS), heads(proj('a_q2'), DA_HEADS),
                          heads(proj('a_k1'), DA_HEADS), heads(proj('a_k2'), DA_HEADS),
                          heads(proj('a_v'), DA_HEADS), lam, lam_init, qn_w, kn_w, subln_w)
    y_b = _hgrn2(heads(proj('b_q'), HG_HEADS), heads(proj('b_f'), HG_HEADS),
                 heads(proj('b_i'), HG_HEADS), heads(proj('b_g'), HG_HEADS), lb, gnorm_w)
    qk = jax.nn.silu(_causal_conv(proj('c_qk'), conv_w, conv_b))
    c_q, c_k = jnp.split(qk, 2, axis=-1)
    y_c = _mlstm(heads(c_q, ML_HEADS), heads(c_k, ML_HEADS), heads(proj('c_v'), ML_HEADS),
                 heads(proj('c_o'), ML_HEADS), proj('c_i') + ib, proj('c_f') + fb, cnorm_w)
    gates = jax.nn.sigmoid(proj('gate')).reshape(B, S, N_BRANCH, D_MODEL)
    merged = (gates[:, :, 0] * (y_a @ w_branch[0])
              + gates[:, :, 1] * (y_b @ w_branch[1])
              + gates[:, :, 2] * (y_c @ w_branch[2]))
    return merged @ w_out

def _moe(h, router_w, router_b, w1, w3, w2):
    f32 = jnp.float32
    logits = (h @ router_w).astype(f32) + router_b.astype(f32)
    probs = jax.nn.softmax(logits, axis=-1)
    top_p, top_i = lax.top_k(probs, TOP_K)
    top_p = top_p / jnp.sum(top_p, axis=-1, keepdims=True)
    combine = jnp.sum(jax.nn.one_hot(top_i, N_EXPERTS, dtype=f32) * top_p[..., None], axis=-2)
    out = jnp.zeros_like(h)
    for e in range(N_EXPERTS):
        out = out + combine[..., e:e + 1].astype(h.dtype) * _swiglu(h, w1[e], w3[e], w2[e])
    return out

def first_inputs(seed: int = 0) -> dict:
    key = jax.random.key(seed)
    ks = jax.random.split(key, 32)
    f32 = jnp.float32
    D = D_MODEL

    def nrm(k, shape, scale):
        return scale * jax.random.normal(k, shape, f32)

    def gain(k, shape):
        return 1.0 + 0.02 * jax.random.normal(k, shape, f32)

    return {
        'x': nrm(ks[0], (BATCH, SEQ, D), 1.0),
        'c': nrm(ks[1], (BATCH, D), 1.0),
        'w_mod': nrm(ks[2], (DEPTH, D, 6 * D), 0.5 * D ** -0.5),
        'b_mod': nrm(ks[3], (DEPTH, 6 * D), 0.02),
        'norm1_w': gain(ks[4], (DEPTH, D)),
        'norm2_w': gain(ks[5], (DEPTH, D)),
        'w_in': nrm(ks[6], (DEPTH, D, D_IN), D ** -0.5),
        'c_conv_w': nrm(ks[7], (DEPTH, ML_CONV, 2 * ML_HEADS * ML_DK), ML_CONV ** -0.5),
        'c_conv_b': nrm(ks[8], (DEPTH, 2 * ML_HEADS * ML_DK), 0.02),
        'a_qnorm_w': gain(ks[9], (DEPTH, DA_DK)),
        'a_knorm_w': gain(ks[10], (DEPTH, DA_DK)),
        'a_lambda_q1': nrm(ks[11], (DEPTH, DA_DK), 0.1),
        'a_lambda_k1': nrm(ks[12], (DEPTH, DA_DK), 0.1),
        'a_lambda_q2': nrm(ks[13], (DEPTH, DA_DK), 0.1),
        'a_lambda_k2': nrm(ks[14], (DEPTH, DA_DK), 0.1),
        'a_subln_w': gain(ks[15], (DEPTH, DA_DV)),
        'b_lb_logits': nrm(ks[16], (DEPTH, HG_HEADS * HG_DK), 1.0),
        'b_gnorm_w': gain(ks[17], (DEPTH, HG_DV)),
        'c_igate_b': nrm(ks[18], (DEPTH, ML_HEADS), 0.1),
        'c_fgate_b': jnp.linspace(3.0, 6.0, ML_HEADS, dtype=f32)[None, :] + nrm(ks[19], (DEPTH, ML_HEADS), 0.1),
        'c_norm_w': gain(ks[20], (DEPTH, ML_DV)),
        'w_branch': nrm(ks[21], (DEPTH, N_BRANCH, BRANCH_W, D), BRANCH_W ** -0.5),
        'w_out': nrm(ks[22], (DEPTH, D, D), D ** -0.5),
        'ffn_w1': nrm(ks[23], (N_DENSE, D, D_FF), D ** -0.5),
        'ffn_w3': nrm(ks[24], (N_DENSE, D, D_FF), D ** -0.5),
        'ffn_w2': nrm(ks[25], (N_DENSE, D_FF, D), D_FF ** -0.5),
        'moe_router_w': nrm(ks[26], (N_MOE, D, N_EXPERTS), D ** -0.5),
        'moe_router_b': nrm(ks[27], (N_MOE, N_EXPERTS), 0.01),
        'moe_w1': nrm(ks[28], (N_MOE, N_EXPERTS, D, D_FF), D ** -0.5),
        'moe_w3': nrm(ks[29], (N_MOE, N_EXPERTS, D, D_FF), D ** -0.5),
        'moe_w2': nrm(ks[30], (N_MOE, N_EXPERTS, D_FF, D), D_FF ** -0.5),
    }

def first_block(x, c, w_mod, b_mod, norm1_w, norm2_w, w_in, c_conv_w, c_conv_b,
              a_qnorm_w, a_knorm_w, a_lambda_q1, a_lambda_k1, a_lambda_q2, a_lambda_k2,
              a_subln_w, b_lb_logits, b_gnorm_w, c_igate_b, c_fgate_b, c_norm_w,
              w_branch, w_out, ffn_w1, ffn_w3, ffn_w2,
              moe_router_w, moe_router_b, moe_w1, moe_w3, moe_w2):
    lb_all = jnp.cumsum(jax.nn.softmax(b_lb_logits.astype(jnp.float32), axis=0), axis=0)
    lb_all = lb_all - lb_all[:1]
    cond = jax.nn.silu(c)
    for l in range(DEPTH):
        mod = cond @ w_mod[l] + b_mod[l]
        sh1, sc1, g1, sh2, sc2, g2 = jnp.split(mod, 6, axis=-1)
        lam_init = 0.8 - 0.6 * math.exp(-0.3 * l)
        h = _modulate(_rmsnorm(x, norm1_w[l]), sh1, sc1)
        y = _mixer(h, w_in[l], c_conv_w[l], c_conv_b[l], a_qnorm_w[l], a_knorm_w[l],
                   a_lambda_q1[l], a_lambda_k1[l], a_lambda_q2[l], a_lambda_k2[l],
                   a_subln_w[l], lam_init, lb_all[l], b_gnorm_w[l],
                   c_igate_b[l], c_fgate_b[l], c_norm_w[l], w_branch[l], w_out[l])
        x = x + g1[:, None, :] * y
        h = _modulate(_rmsnorm(x, norm2_w[l]), sh2, sc2)
        if l % 2 == 0:
            i = l // 2
            y = _swiglu(h, ffn_w1[i], ffn_w3[i], ffn_w2[i])
        else:
            i = l // 2
            y = _moe(h, moe_router_w[i], moe_router_b[i], moe_w1[i], moe_w3[i], moe_w2[i])
        x = x + g2[:, None, :] * y
    return x


HEAD_DIM = 64
N_HEADS = D_MODEL // HEAD_DIM
INNER = N_HEADS * HEAD_DIM
ROT_DIM = HEAD_DIM // 4
ROPE_THETA = 500000.0
DSWA_GROUPS = ((128, 1), (512, 4), (2048, 16))
N_GROUPS = len(DSWA_GROUPS)
BLOCK = 128
N_MIXERS = 2
EPS = 1e-6
FOX_IN = 4 * INNER + N_HEADS
DSW_IN = 3 * N_GROUPS * INNER + INNER


def rms_norm(x, g):
    xf = x.astype(jnp.float32)
    y = xf * lax.rsqrt(jnp.mean(xf * xf, axis=-1, keepdims=True) + EPS) * g.astype(jnp.float32)
    return y.astype(x.dtype)

def rotary_tables(positions):
    inv_freq = ROPE_THETA ** (-jnp.arange(0, ROT_DIM, 2, dtype=jnp.float32) / ROT_DIM)
    ang = positions.astype(jnp.float32)[..., None] * inv_freq
    return jnp.cos(ang), jnp.sin(ang)

def apply_partial_rotary(t, cos, sin):
    half = ROT_DIM // 2
    c = cos[:, :, None, None, :].astype(t.dtype)
    s = sin[:, :, None, None, :].astype(t.dtype)
    t1, t2, rest = t[..., :half], t[..., half:ROT_DIM], t[..., ROT_DIM:]
    return jnp.concatenate([t1 * c - t2 * s, t2 * c + t1 * s, rest], axis=-1)

def fox_attention(q, k, v, c):
    B, S, H, dh = q.shape
    nq = S // BLOCK
    scale = dh ** -0.5
    qb = q.reshape(B, nq, BLOCK, H, dh).transpose(1, 0, 2, 3, 4)
    cb = c.reshape(B, nq, BLOCK, H).transpose(1, 0, 3, 2)
    c_k = c.transpose(0, 2, 1)
    key_pos = jnp.arange(S)

    def one_block(args):
        qi, ci, bi = args
        s = jnp.einsum('bqhd,bkhd->bhqk', qi, k).astype(jnp.float32) * scale
        s = s + ci[..., None] - c_k[:, :, None, :]
        q_pos = bi * BLOCK + jnp.arange(BLOCK)
        mask = key_pos[None, :] <= q_pos[:, None]
        s = jnp.where(mask, s, -jnp.inf)
        p = jax.nn.softmax(s, axis=-1).astype(v.dtype)
        return jnp.einsum('bhqk,bkhd->bqhd', p, v)

    o = lax.map(one_block, (qb, cb, jnp.arange(nq)))
    return o.transpose(1, 0, 2, 3, 4).reshape(B, S, H, dh)

def fox_mixer(h, w_in, b_f, q_g, k_g):
    B, S, _ = h.shape
    proj = h @ w_in
    q = rms_norm(proj[..., :INNER].reshape(B, S, N_HEADS, HEAD_DIM), q_g)
    k = rms_norm(proj[..., INNER:2 * INNER].reshape(B, S, N_HEADS, HEAD_DIM), k_g)
    v = proj[..., 2 * INNER:3 * INNER].reshape(B, S, N_HEADS, HEAD_DIM)
    gate = proj[..., 3 * INNER:4 * INNER]
    f_logit = proj[..., 4 * INNER:].astype(jnp.float32) + b_f.astype(jnp.float32)
    c = jnp.cumsum(jax.nn.log_sigmoid(f_logit), axis=1)
    o = fox_attention(q, k, v, c)
    return o.reshape(B, S, INNER), gate

def _band(t):
    prev = jnp.concatenate([jnp.zeros_like(t[:, :1]), t[:, :-1]], axis=1)
    return jnp.concatenate([prev, t], axis=2)

def dilated_window_attention(q, k, v, window, dilation):
    B, S, H, dh = q.shape
    r = dilation
    L = S // r
    n_back = window // r
    nb = -(-L // BLOCK)
    Lp = nb * BLOCK
    scale = dh ** -0.5

    def to_blocks(t):
        t = t.reshape(B, L, r, H, dh).transpose(0, 2, 1, 3, 4).reshape(B * r, L, H, dh)
        t = jnp.pad(t, ((0, 0), (0, Lp - L), (0, 0), (0, 0)))
        return t.reshape(B * r, nb, BLOCK, H, dh)

    qb, kb, vb = to_blocks(q), to_blocks(k), to_blocks(v)
    s = jnp.einsum('znqhd,znkhd->znhqk', qb, _band(kb)).astype(jnp.float32) * scale
    q_idx = jnp.arange(nb)[:, None] * BLOCK + jnp.arange(BLOCK)[None, :]
    k_idx = jnp.arange(nb)[:, None] * BLOCK - BLOCK + jnp.arange(2 * BLOCK)[None, :]
    dist = q_idx[:, :, None] - k_idx[:, None, :]
    mask = (dist >= 0) & (dist <= n_back) & (k_idx[:, None, :] >= 0)
    s = jnp.where(mask[None, :, None], s, -jnp.inf)
    lse = jax.nn.logsumexp(s, axis=-1)
    p = jnp.exp(s - lse[..., None]).astype(v.dtype)
    o = jnp.einsum('znhqk,znkhd->znqhd', p, _band(vb))
    o = o.reshape(B * r, Lp, H, dh)[:, :L]
    o = o.reshape(B, r, L, H, dh).transpose(0, 2, 1, 3, 4).reshape(B, S, H, dh)
    lse = lse.transpose(0, 1, 3, 2).reshape(B * r, Lp, H)[:, :L]
    lse = lse.reshape(B, r, L, H).transpose(0, 2, 1, 3).reshape(B, S, H)
    return o, lse

def dsw_mixer(h, cos, sin, w_in, q_g, k_g):
    B, S, _ = h.shape
    proj = h @ w_in
    qkv = proj[..., :3 * N_GROUPS * INNER].reshape(B, S, 3, N_GROUPS, N_HEADS, HEAD_DIM)
    gate = proj[..., 3 * N_GROUPS * INNER:]
    q = apply_partial_rotary(rms_norm(qkv[:, :, 0], q_g[:, None, :]), cos, sin)
    k = apply_partial_rotary(rms_norm(qkv[:, :, 1], k_g[:, None, :]), cos, sin)
    v = qkv[:, :, 2]
    outs, lses = [], []
    for g, (window, dilation) in enumerate(DSWA_GROUPS):
        o_g, lse_g = dilated_window_attention(q[:, :, g], k[:, :, g], v[:, :, g], window, dilation)
        outs.append(o_g)
        lses.append(lse_g)
    wts = jax.nn.softmax(jnp.stack(lses, axis=0), axis=0).astype(v.dtype)
    o = jnp.einsum('gbsh,gbshd->bshd', wts, jnp.stack(outs, axis=0))
    return o.reshape(B, S, INNER), gate

def second_inputs(seed: int = 0) -> dict:
    key = jax.random.key(seed)
    ks = jax.random.split(key, 13)
    n_fox = (DEPTH + 1) // N_MIXERS
    n_dsw = DEPTH // N_MIXERS
    f32 = jnp.float32
    x = jax.random.normal(ks[0], (BATCH, SEQ, D_MODEL), f32)
    offset = jax.random.randint(ks[1], (BATCH, 1), 0, 4096, dtype=jnp.int32)
    positions = offset + jnp.arange(SEQ, dtype=jnp.int32)[None, :]
    norm_g = 1.0 + 0.02 * jax.random.normal(ks[2], (DEPTH, D_MODEL), f32)
    fox_w_in = jax.random.normal(ks[3], (n_fox, D_MODEL, FOX_IN), f32) * D_MODEL ** -0.5
    fox_b_f = jax.random.uniform(ks[4], (n_fox, N_HEADS), f32, minval=1.0, maxval=4.0)
    fox_q_norm = 1.0 + 0.02 * jax.random.normal(ks[5], (n_fox, HEAD_DIM), f32)
    fox_k_norm = 1.0 + 0.02 * jax.random.normal(ks[6], (n_fox, HEAD_DIM), f32)
    fox_w_out = jax.random.normal(ks[7], (n_fox, INNER, D_MODEL), f32) * (2 * INNER) ** -0.5
    dsw_w_in = jax.random.normal(ks[8], (n_dsw, D_MODEL, DSW_IN), f32) * D_MODEL ** -0.5
    dsw_q_norm = 1.0 + 0.02 * jax.random.normal(ks[9], (n_dsw, N_GROUPS, HEAD_DIM), f32)
    dsw_k_norm = 1.0 + 0.02 * jax.random.normal(ks[10], (n_dsw, N_GROUPS, HEAD_DIM), f32)
    dsw_w_out = jax.random.normal(ks[11], (n_dsw, INNER, D_MODEL), f32) * (2 * INNER) ** -0.5
    return {"x": x, "positions": positions, "norm_g": norm_g,
            "fox_w_in": fox_w_in, "fox_b_f": fox_b_f, "fox_q_norm": fox_q_norm,
            "fox_k_norm": fox_k_norm, "fox_w_out": fox_w_out,
            "dsw_w_in": dsw_w_in, "dsw_q_norm": dsw_q_norm, "dsw_k_norm": dsw_k_norm,
            "dsw_w_out": dsw_w_out}

def second_block(x, positions, norm_g, fox_w_in, fox_b_f, fox_q_norm, fox_k_norm, fox_w_out,
              dsw_w_in, dsw_q_norm, dsw_k_norm, dsw_w_out):
    cos, sin = rotary_tables(positions)
    for i in range(DEPTH):
        j = i // N_MIXERS
        h = rms_norm(x, norm_g[i])
        if i % N_MIXERS == 0:
            o, gate = fox_mixer(h, fox_w_in[j], fox_b_f[j], fox_q_norm[j], fox_k_norm[j])
            w_out = fox_w_out[j]
        else:
            o, gate = dsw_mixer(h, cos, sin, dsw_w_in[j], dsw_q_norm[j], dsw_k_norm[j])
            w_out = dsw_w_out[j]
        x = x + (o * jax.nn.silu(gate)) @ w_out
    return x


def setup_inputs(seed=0):
    out = dict(first_inputs(seed))
    for name, value in second_inputs(seed + 1).items():
        if name != "x":
            out[name + "_2"] = value
    return out


def reference(
    x, c, w_mod, b_mod, norm1_w, norm2_w, w_in, c_conv_w, c_conv_b, a_qnorm_w, a_knorm_w,
    a_lambda_q1, a_lambda_k1, a_lambda_q2, a_lambda_k2, a_subln_w, b_lb_logits, b_gnorm_w,
    c_igate_b, c_fgate_b, c_norm_w, w_branch, w_out, ffn_w1, ffn_w3, ffn_w2, moe_router_w,
    moe_router_b, moe_w1, moe_w3, moe_w2, positions_2, norm_g_2, fox_w_in_2, fox_b_f_2,
    fox_q_norm_2, fox_k_norm_2, fox_w_out_2, dsw_w_in_2, dsw_q_norm_2, dsw_k_norm_2,
    dsw_w_out_2,
):
    x = first_block(
        x, c, w_mod, b_mod, norm1_w, norm2_w, w_in, c_conv_w, c_conv_b, a_qnorm_w, a_knorm_w,
        a_lambda_q1, a_lambda_k1, a_lambda_q2, a_lambda_k2, a_subln_w, b_lb_logits, b_gnorm_w,
        c_igate_b, c_fgate_b, c_norm_w, w_branch, w_out, ffn_w1, ffn_w3, ffn_w2, moe_router_w,
        moe_router_b, moe_w1, moe_w3, moe_w2,
    )
    return second_block(
        x, positions_2, norm_g_2, fox_w_in_2, fox_b_f_2, fox_q_norm_2, fox_k_norm_2,
        fox_w_out_2, dsw_w_in_2, dsw_q_norm_2, dsw_k_norm_2, dsw_w_out_2,
    )


_drawn_inputs = setup_inputs


def setup_inputs(seed=0):
    import zlib

    import numpy as np

    out = dict(_drawn_inputs(seed))
    spreads = {}
    factors = {'norm1_w': 4.677,
     'norm2_w': 2.999,
     'c_conv_b': 6.889,
     'a_qnorm_w': 8.0,
     'a_knorm_w': 7.431,
     'a_lambda_q1': 4.753,
     'a_lambda_k1': 4.701,
     'a_lambda_q2': 5.926,
     'a_lambda_k2': 5.13,
     'a_subln_w': 8.0,
     'b_lb_logits': 3.675,
     'b_gnorm_w': 8.0,
     'c_igate_b': 64.0,
     'c_norm_w': 8.0,
     'moe_router_b': 6.972,
     'norm_g_2': 8.0,
     'fox_q_norm_2': 8.0,
     'fox_k_norm_2': 8.0,
     'dsw_q_norm_2': 8.0,
     'dsw_k_norm_2': 8.0}
    for name, (base, spread) in spreads.items():
        noise = np.random.default_rng([zlib.crc32(name.encode()), seed]).standard_normal(out[name].shape)
        drawn = base * np.exp(spread * noise) if base else spread * noise
        out[name] = __import__('jax').numpy.asarray(drawn.astype(out[name].dtype))
    for name, factor in factors.items():
        out[name] = (out[name] * factor).astype(out[name].dtype)
    return out
```

```python
import math
from contextlib import ExitStack, contextmanager

import numpy as np

import concourse.bass as bass
from concourse import mybir

F32 = mybir.dt.float32
I32 = mybir.dt.int32
ACT = mybir.ActivationFunctionType
ALU = mybir.AluOpType
X = mybir.AxisListType.X

P = 128
D = 1024
KC = D // P
T = 2
S = T * P
DEPTH = 2
UNIT = 2048
UC = UNIT // KC
RING = 11
RING_MIX = 7
D_FF = 2816
FG = D_FF // UC
NE = 8
EXPERT_UNITS = 3 * FG
EPS = 1e-6
NEG = -1e30
HEADS = 4
AK = 64
HD = 128
SLOPES = [2.0 ** (-8.0 * i / HEADS) for i in range(1, HEADS + 1)]
LEVELS = [64, 32, 16, 8, 4, 2, 1]
QUADS = 4
DG = 3
DILATIONS = (1, 4, 16)
ROT = 8
CV = HD + 1

W_IN_A = [(0, 1024), (1024, 1536)]
W_IN_B = [(2048, 2560), (1536, 2048), (2560, 3584)]
W_IN_C = [(3584, 4608), (4608, 5632)]
W_IN_IF = 5632
W_IN_GATE = 5640

COLS = {}
for _name, _n in [("c", KC), ("bmod", 2 * 48), ("n1", 2 * KC), ("n2", 2 * KC), ("router", KC * NE),
                  ("convw", 2 * 32), ("convb", 2 * 8), ("aq", 2), ("ak", 2), ("subln", 2), ("gnorm", 2),
                  ("cnorm", 2), ("lb", 2 * HEADS), ("wif", 2 * KC * 8), ("ng", 2 * KC), ("foxwf", KC * 16),
                  ("foxq", 1), ("foxk", 1), ("ib", 2), ("fb", 2)]:
    COLS[_name] = (sum(n for _, n in COLS.values()), _n)
N_COLS = sum(n for _, n in COLS.values())
ROWS = {}
for _name, _n in [("lam", 2 * 4 * AK), ("rb", NE), ("foxbf", 16), ("dswg", 2 * DG * 64)]:
    ROWS[_name] = (sum(n for _, n in ROWS.values()), _n)
N_ROWS = sum(n for _, n in ROWS.values())


def stream_plan():
    def mixer(l):
        u = [("mod", l, j) for j in range(24)]
        u += [("a", l, j) for j in range(6)] + [("b", l, j) for j in range(8)]
        u += [("c", l, j) for j in range(8)]
        for br in range(3):
            u += [("gate", l, 4 * br + j) for j in range(4)] + [("branch", l, 2 * br + j) for j in range(2)]
        return u + [("out", l, j) for j in range(4)]

    def ffn(name, e):
        u = [("w1" + name, e, 0), ("w3" + name, e, 0)]
        for g in range(1, FG):
            u += [("w1" + name, e, g), ("w3" + name, e, g), ("w2" + name, e, g - 1)]
        return u + [("w2" + name, e, FG - 1)]

    before = mixer(0) + ffn("f", 0) + mixer(1)
    experts = [u for e in range(NE) for u in ffn("m", e)]
    after = [("fox", 0, j) for j in range(4 * QUADS)] + [("foxo", 0, j) for j in range(4)]
    after += [("dsw", 0, j) for j in range((3 * DG + 1) * QUADS)] + [("dswo", 0, j) for j in range(4)]
    return before, experts, after


def ring_plan():
    before, experts, after = stream_plan()
    fills, last, out = [0] * RING, [None] * RING, []
    at = 0
    for name, _, _ in before + experts + after:
        n = RING if name[:2] in ("w1", "w2", "w3") else RING_MIX
        if out and n != kind:
            at = 0
        kind, s = n, at % n
        fills[s] += 1
        out.append((s, fills[s], last[s]))
        last[s] = len(out) - 1
        at += 1
    return out


class Count:

    def __init__(self, sem):
        self.sem, self.n, self.turn = sem, 0, 0

    def more(self, n=1):
        self.n += n
        return self.sem, self.n + self.turn

    def at(self, n):
        return self.sem, n + self.turn


@contextmanager
def turns(eng, times, per):
    with eng.Fori(0, times) as i:
        start = {c: c.n for c in per}
        for c, n in per.items():
            c.turn = i * n
        yield i
        for c, n in per.items():
            assert c.n - start[c] == n, (c.sem, c.n - start[c], n)
            c.turn, c.n = 0, start[c] + n * times


def two_blocks(nc, stream, cols_d, rows_d, bgate_d, x_d, pos_d, out_d, stop=None):
    n_before, n_experts, n_after = (len(u) for u in stream_plan())
    plan = ring_plan()
    ctx = ExitStack()
    with ctx:
        def sb(name, *shape, dt=F32):
            return ctx.enter_context(nc.sbuf_tensor(name, list(shape), dt))

        def sem(name):
            return ctx.enter_context(nc.semaphore(name))

        ring = sb("ring", P, RING, UNIT)
        W = ring[:, RING_MIX:RING, :].rearrange("p a b -> p (a b)")
        x = sb("x_rows", P, T, D)
        hT = sb("hT", P, KC, S)
        RW = 2560
        RA = sb("RA", P, T, RW)
        RB = sb("RB", P, T, RW)
        YT = sb("YT", P, 3, HEADS, S)
        gates_row = sb("gates_row", P, 2, D)
        colt = sb("colt", P, N_COLS)
        rowt = sb("rowt", P, N_ROWS)
        ident = sb("ident", P, P)
        ones = sb("ones", P, P)
        tri = sb("tri", P, P)
        causal = sb("causal", P, S)
        causalT = sb("causalT", P, P)
        dist = sb("dist", P, S)
        lev = sb("lev", P, len(LEVELS), P)
        dmask = sb("dmask", P, DG, S)
        sel = sb("sel", HEADS, HEADS, P)
        cond = sb("cond", P, KC)
        modc = sb("modc", P, 48)
        A1 = sb("A1", P, KC)
        A2 = sb("A2", P, KC)
        junk = sb("junk", P, P)
        small = sb("small", P, 512)
        lamt = sb("lamt", P, 8)
        lbc = sb("lbc", P, 6, HEADS)
        qc66 = sb("qc66", P, 2)
        aT_sb = sb("aT_sb", P, 2, P)
        comb = sb("comb", P, T, NE)
        cosr = sb("cosr", P, T, ROT)
        sinr = sb("sinr", P, T, ROT)
        posi = sb("posi", P, T, dt=I32)
        idx = sb("idx", P, S, dt=I32)
        idx2 = sb("idx2", P, S, dt=I32)
        negS = small[:, 192:200]
        sumS = small[:, 200:208]
        recS = small[:, 208:216]
        meansq = small[:, 128:176]
        ssx = small[:, 448:450]
        ps = ctx.enter_context(nc.psum_tensor("ps", [P, 8, 512], F32))
        psS = [ps[:, 4:6, :].rearrange("p a b -> p (a b)"), ps[:, 6:8, :].rearrange("p a b -> p (a b)")]

        def col(name, lo=0, n=1):
            o = COLS[name][0] + lo
            return colt[:, o:o + n]

        def row(name):
            o, n = ROWS[name]
            return rowt[:, o:o + n]

        landed = [sem(f"landed{s}") for s in range(RING)]
        unit_done = sem("unit_done")
        burst_for_dve = sem("burst_for_dve")
        burst_for_act = sem("burst_for_act")
        dve_took = sem("dve_took")
        act_took = sem("act_took")
        dve_gave_pe = sem("dve_gave_pe")
        act_gave_pe = sem("act_gave_pe")
        dve_gave_act = sem("dve_gave_act")
        act_gave_dve = sem("act_gave_dve")
        dve_step = sem("dve_step")
        act_step = sem("act_step")
        pool_step = sem("pool_step")
        masks_made = sem("masks_made")
        inputs_in = sem("inputs_in")
        bgate_in = sem("bgate_in")
        work_free = sem("work_free")
        gates_free = sem("gates_free")
        out_ready = sem("out_ready")
        out_written = sem("out_written")

        ticket = {}

        stages = ["mix0", "ffn0", "mix1", "moe", "fox", "dsw"]
        last = stages.index(stop) if stop else len(stages) - 1

        full = {}

        def bank_of(eng, key, turn=None):
            bank, s, v, per = full[key]
            eng.wait_ge(s, v if turn is None else turn * per + v)
            return bank

        A_QT = W[:, 0:2048].rearrange("p (b s) -> p b s", b=8)
        A_SQ = W[:, 2048:3072]
        A_S = W[:, 4096:4608]
        A_E = W[:, 4608:5120]
        A_W = W[:, 5120:5632].rearrange("p (n k) -> p n k", n=2)
        Y_A = W[:, 5632:6656].rearrange("p (t h d) -> p t h d", t=T, h=HEADS)

        def heads_T(a):
            return W[:, a:a + 1024].rearrange("p (h s) -> p h s", h=HEADS)

        B_Q, B_K, B_B, B_E, B_QP, B_KP = (heads_T(1024 * i) for i in range(6))
        B_ATT = W[:, 6144:7168].rearrange("p (t h s) -> p t h s", t=T, h=HEADS)
        B_ATTX = W[:, 7168:7680].rearrange("p (h s) -> p h s", h=HEADS)
        B_TMP = W[:, 7680:8192]
        Y_B = W[:, 0:1024].rearrange("p (t h d) -> p t h d", t=T, h=HEADS)
        C_PAD = W[:, 0:2080].rearrange("p (b s) -> p b s", b=8)
        C_M = heads_T(0)
        C_QK = W[:, 2080:4128].rearrange("p (b s) -> p b s", b=8)
        C_R4, C_EM4, C_M4 = (W[0:4, a:a + S] for a in (4608, 4864, 5120))
        C_F4, C_B4, C_I4 = (W[0:4, a:a + S] for a in (6528, 6784, 7168))
        C_G, C_E, C_W = (W[:, a:a + 384] for a in (5376, 5760, 6144))
        Y_C = W[:, 7168:8192].rearrange("p (t h d) -> p t h d", t=T, h=HEADS)
        D_S = [W[:, a:a + 768].rearrange("p (g k) -> p g k", g=DG) for a in (3104, 3872)]
        PR = [W[:, a:a + 768].rearrange("p (g k) -> p g k", g=DG) for a in (4864, 5632)]
        PT = W[:, 6400:7168].rearrange("p (k g q) -> p k g q", k=T, g=DG)
        D_SQ = W[:, 3104:4640]
        F_QA = W[:, 0:1056].rearrange("p (t v d) -> p t v d", t=T, v=8)
        F_QT = W[:, 1056:3104].rearrange("p (v s) -> p v s", v=8)
        D_QT = W[:, 0:3072].rearrange("p (v s) -> p v s", v=12)
        OG = YT[:, :, :, :].rearrange("p b h s -> p (b h s)")[:, 0:T * D].rearrange("p (t d) -> p t d", t=T)
        gate_h = RA[:, 0, 0:1024].rearrange("p (n c) -> p n c", n=2)
        hid = RA[:, 0, 1024:2048].rearrange("p (n t c) -> p n t c", n=2, t=T)
        actT = RA[:, 1, 0:1024].rearrange("p (n k s) -> p n k s", n=2, k=2)
        moe_sum = RB[:, :, 1024:2048]

        def want(stage):
            return stages.index(stage) <= last

        ATT = [(t, h) for t in range(T) for h in range(4)]

        block = ctx.enter_context(nc.Block())

        @block.tensor
        def _(pe):
            done = Count(unit_done)
            for_dve, for_act = Count(burst_for_dve), Count(burst_for_act)
            took = {"dve": Count(dve_took), "act": Count(act_took)}
            from_dve, from_act = Count(dve_gave_pe), Count(act_gave_pe)
            freed = {}
            state = {"unit": 0, "U": 0, "T": 0, "S": 0}

            def free(bank):
                if bank in freed:
                    c, n = freed[bank]
                    pe.wait_ge(*c.at(n))

            def taken_by(who, banks, key):
                c = took[who]
                c.more()
                for b in banks:
                    freed[b] = (c, c.n)
                ticket[key] = (who, c.n)

            def need(key):
                who, n = ticket[key]
                pe.wait_ge(*took[who].at(n))

            def next_bank(kind):
                banks = {"U": [0, 1], "T": [2, 3], "S": [4, 6]}[kind]
                b = banks[state[kind] % 2]
                state[kind] += 1
                free(b)
                if kind == "S":
                    free(b + 1)
                return b

            def landed_unit(turn=None, base_fill=None):
                u = state["unit"]
                state["unit"] += 1
                s, fill, _ = plan[u]
                if turn is None:
                    pe.wait_ge(landed[s], 16 * fill)
                else:
                    pe.wait_ge(landed[s], turn * (16 * 3) + 16 * fill)
                return s

            def rows_unit(who, key, turn=None, tiles=T, lhs=None):
                lhs = hT if lhs is None else lhs
                s = landed_unit(turn)
                b = next_bank("U")
                for t in range(tiles):
                    for k in range(KC):
                        m = pe.matmul(ps[:, b, t * UC:(t + 1) * UC], lhs[:, k, t * P:(t + 1) * P],
                                      ring[:, s, k * UC:(k + 1) * UC], start=k == 0, stop=k == KC - 1)
                m.then_inc(unit_done, 1)
                unit_full(who, [b], key)

            def unit_full(who, banks, key):
                done.more()
                full[key] = (banks[0], unit_done, done.n, EXPERT_UNITS)
                taken_by(who, banks, key)

            def finish(m, who, banks, key):
                c, sem_ = (for_dve, burst_for_dve) if who == "dve" else (for_act, burst_for_act)
                c.more()
                m.then_inc(sem_, 1)
                full[key] = (banks[0], sem_, c.n, FG)
                taken_by(who, banks, key)

            def transposes(who, key, ins, width=P):
                b = next_bank("T")
                for i, a in enumerate(ins):
                    m = pe.transpose(ps[0:width, b, i * P:(i + 1) * P], a, ident[:, :])
                finish(m, who, [b], key)

            def norm_T(tag, src):
                for t in range(T):
                    pe.wait_ge(*from_dve.more())
                    for g in range(2):
                        transposes("dve", (tag, t, g),
                                   [src[:, t, (4 * g + i) * P:(4 * g + i + 1) * P] for i in range(4)])
                need((tag, T - 1, 1))

            def mod(l):
                pe.wait_ge(*from_dve.more())
                cb = RA[:, 0, 0:KC * P].rearrange("p (k n) -> p k n", k=KC)
                for j in range(24):
                    s = landed_unit()
                    b = next_bank("U")
                    for k in range(KC):
                        m = pe.matmul(ps[:, b, 0:UC], cb[:, k, :], ring[:, s, k * UC:(k + 1) * UC],
                                      start=k == 0, stop=k == KC - 1)
                    m.then_inc(unit_done, 1)
                    unit_full("dve", [b], ("mod", l, j))

            def diff_attention(l):
                QT = A_QT
                for t in range(T):
                    pe.wait_ge(*from_dve.more())
                    for g in range(2):
                        transposes("dve", ("aT", l, t, g),
                                   [RA[:, t, (4 * g + i) * P:(4 * g + i + 1) * P] for i in range(4)])
                need(("aT", l, T - 1, 1))
                for t in range(T):
                    nk = (t + 1) * P

                    def score(h):
                        b = next_bank("S")
                        r = 64 * (h % 2)
                        for m_ in range(2):
                            m = pe.matmul(ps[:, b, m_ * nk:(m_ + 1) * nk],
                                          QT[r:r + AK, 2 * m_ + h // 2, t * P:(t + 1) * P],
                                          QT[r:r + AK, 4 + 2 * m_ + h // 2, 0:nk], start=True, stop=True)
                        finish(m, "dve", [b], ("aS", l, t, h))

                    score(0)
                    bo = 5 + 2 * t
                    for h in range(HEADS):
                        if h + 1 < HEADS:
                            score(h + 1)
                        pe.wait_ge(*from_dve.more())
                        a = A_W[:, h % 2, :]
                        transposes("act", ("aA", l, t, h), [a[:, i * P:(i + 1) * P] for i in range(t + 1)])
                        need(("aA", l, t, h))
                        if h == 0:
                            free(bo)
                        for kt in range(t + 1):
                            m = pe.matmul(ps[:, bo, h * HD:(h + 1) * HD], aT_sb[:, kt, :],
                                          RA[:, kt, 1024 + h * HD:1024 + (h + 1) * HD],
                                          start=kt == 0, stop=kt == t)
                    finish(m, "dve", [bo], ("aO", l, t))

            def y_T(l, br):
                for t in range(T):
                    pe.wait_ge(*from_dve.more())
                    transposes("dve", ("yT", l, br, t), [(Y_A, Y_B, Y_C)[br][:, t, i, :] for i in range(4)])

            def hgrn(l):
                Qb, Kb, Qp, Kp, att, attx = B_Q, B_K, B_QP, B_KP, B_ATT, B_ATTX
                for i in range(2):
                    for t in range(T):
                        transposes("act", ("bT", l, i, t),
                                   [RB[:, t, 512 * i + j * P:512 * i + (j + 1) * P] for j in range(4)])
                for n in range(len(LEVELS) + 1):
                    pe.wait_ge(*from_dve.more())
                    q, k = (Qb, Kb) if n == 0 else (Qp, Kp)
                    for t in range(T):
                        b = next_bank("S")
                        for h in range(HEADS):
                            m = pe.matmul(ps[:, b, h * P:(h + 1) * P], k[:, h, t * P:(t + 1) * P],
                                          q[:, h, t * P:(t + 1) * P], start=True, stop=True)
                        finish(m, "dve", [b, b + 1], ("lev", l, n, t))
                pe.wait_ge(*from_dve.more())
                b = next_bank("S")
                for h in range(HEADS):
                    m = pe.matmul(ps[:, b, h * P:(h + 1) * P], Kp[:, h, 0:P], Qp[:, h, P:S],
                                  start=True, stop=True)
                finish(m, "dve", [b, b + 1], ("levx", l))
                need(("levx", l))
                for t in range(T):
                    b = next_bank("S")
                    for h in range(HEADS):
                        o = ps[:, b, h * HD:(h + 1) * HD]
                        vv = lambda t_: RB[:, t_, 1024 + h * HD:1024 + (h + 1) * HD]
                        m = pe.matmul(o, att[:, t, h, :], vv(t), start=True, stop=t == 0)
                        if t == 1:
                            m = pe.matmul(o, attx[:, h, :], vv(0), start=False, stop=True)
                    finish(m, "dve", [b, b + 1], ("bO", l, t))

            def gate_logits(l):
                b = next_bank("T")
                for i in range(2):
                    for k in range(KC):
                        w = col("wif", (l * KC + k) * 8 + 4 * i, 4)
                        m = pe.matmul(ps[0:4, b, i * S:(i + 1) * S], w, hT[:, k, :],
                                      start=k == 0, stop=k == KC - 1)
                finish(m, "dve", [b], ("cG", l))

            def mlstm(l):
                gate_logits(l)
                QK, r4, em4, M4 = C_QK, C_R4, C_EM4, C_M4
                for t in range(T):
                    for g in range(2):
                        transposes("act", ("cT", l, t, g),
                                   [RA[:, t, (4 * g + i) * P:(4 * g + i + 1) * P] for i in range(4)])
                pe.wait_ge(*from_act.more())
                b = next_bank("T")
                for i, a in enumerate((r4, em4)):
                    for t in range(T):
                        m = pe.transpose(ps[:, b, (2 * i + t) * 4:(2 * i + t) * 4 + 4],
                                         a[:, t * P:(t + 1) * P], ident[0:4, 0:4])
                finish(m, "dve", [b], ("cR", l))
                for hp in range(2):
                    b = next_bank("T")
                    for i in range(2):
                        m = pe.matmul(ps[:, b, i * S:(i + 1) * S], sel[:, 2 * hp + i, :], M4,
                                      start=True, stop=True)
                    finish(m, "dve", [b], ("cM", l, hp))
                pe.wait_ge(*from_act.more())
                for h in range(HEADS):
                    b = next_bank("S")
                    pe.matmul(ps[:, b, 0:S], QK[:, 4 + h, 0:P], QK[:, h, :], start=True, stop=True)
                    m = pe.matmul(ps[:, b, S:S + P], QK[:, 4 + h, P:S], QK[:, h, P:S], start=True, stop=True)
                    finish(m, "dve", [b, b + 1], ("cw", l, h))
                    need(("cw", l, h))
                    Wt = C_W
                    vv = lambda t_: RA[:, t_, 1024 + h * CV:1024 + (h + 1) * CV]
                    b = next_bank("T")
                    pe.matmul(ps[:, b, 0:CV], Wt[:, 0:P], vv(0), start=True, stop=True)
                    pe.matmul(ps[:, b, 256:256 + CV], Wt[:, P:2 * P], vv(0), start=True, stop=False)
                    m = pe.matmul(ps[:, b, 256:256 + CV], Wt[:, 2 * P:3 * P], vv(1), start=False, stop=True)
                    finish(m, "dve", [b], ("cO", l, h))

            def merge(l, br):
                for j in range(4):
                    rows_unit("act", ("gate", l, br, j))
                if br == 0:
                    for b_ in range(3):
                        need(("yT", l, b_, T - 1))
                for j in range(2):
                    s = landed_unit()
                    b = next_bank("S")
                    for t in range(T):
                        for k in range(4):
                            m = pe.matmul(ps[:, b + t, :], YT[:, br, k, t * P:(t + 1) * P],
                                          ring[:, s, k * 512:(k + 1) * 512], start=k == 0, stop=k == 3)
                    m.then_inc(unit_done, 1)
                    unit_full("dve", [b, b + 1], ("branch", l, br, j))

            def project(tag, src_ready):
                for t in range(T):
                    pe.wait_ge(*from_dve.more())
                    for g in range(2):
                        transposes("act", (tag, t, g), [src_ready(t, 4 * g + i) for i in range(4)])
                need((tag, T - 1, 1))
                for j in range(4):
                    rows_unit("dve", (tag + "o", j))

            def mixer(l):
                if l == 0:
                    pe.wait_ge(masks_made, 1)
                mod(l)
                norm_T(f"n1{l}", RB)
                for j in range(6):
                    rows_unit("act", ("a", l, j))
                for j in range(8):
                    rows_unit("act", ("b", l, j))
                diff_attention(l)
                y_T(l, 0)
                for j in range(8):
                    rows_unit("act", ("c", l, j))
                hgrn(l)
                y_T(l, 1)
                mlstm(l)
                y_T(l, 2)
                for br in range(3):
                    merge(l, br)
                project(f"m{l}", lambda t, i: RA[:, t, i * P:(i + 1) * P])

            def swiglu(l, turn=None):
                def down(g):
                    s = landed_unit(turn)
                    need(("act", l, g))
                    for t in range(T):
                        for n in range(2):
                            if g == 0:
                                free(4 + 2 * t + n)
                            for k in range(2):
                                m = pe.matmul(ps[:, 4 + 2 * t + n, :], actT[:, g % 2, k, t * P:(t + 1) * P],
                                              ring[:, s, k * D + n * 512:k * D + n * 512 + 512],
                                              start=g == 0 and k == 0, stop=g == FG - 1 and k == 1)
                    m.then_inc(unit_done, 1)
                    done.more()
                    full["y", l] = (4, unit_done, done.n, EXPERT_UNITS)

                def turn_rows(g):
                    need(("w3", l, g))
                    transposes("act", ("act", l, g), [hid[:, g % 2, t, k * P:(k + 1) * P]
                                                   for k in range(2) for t in range(T)])

                for g in range(FG):
                    rows_unit("act", ("w1", l, g), turn)
                    rows_unit("dve", ("w3", l, g), turn)
                    if g >= 1:
                        turn_rows(g - 1)
                        down(g - 1)
                turn_rows(FG - 1)
                down(FG - 1)
                for t in range(T):
                    taken_by("dve", [4 + 2 * t, 5 + 2 * t], ("y", l, t))

            def ffn(l):
                norm_T(f"n2{l}", RB)
                if l == 0:
                    swiglu(l)
                    return
                b = next_bank("T")
                for t in range(T):
                    for k in range(KC):
                        m = pe.matmul(ps[:, b, t * NE:(t + 1) * NE], hT[:, k, t * P:(t + 1) * P],
                                      col("router", k * NE, NE), start=k == 0, stop=k == KC - 1)
                finish(m, "dve", [b], "router")
                state["U"] = state["T"] = 0
                for b in range(4):
                    pe.wait_ge(*took["dve"].at(took["dve"].n))
                    pe.wait_ge(*took["act"].at(took["act"].n))
                    freed.pop(b, None)
                d0, a0 = took["dve"].n, took["act"].n
                with turns(pe, NE, {done: EXPERT_UNITS, for_act: FG, took["dve"]: FG + T,
                                    took["act"]: 2 * FG}) as i:
                    u0 = state["unit"]
                    freed[0] = (took["act"], a0)
                    freed[1] = (took["dve"], d0 - T)
                    freed[2] = freed[3] = (took["act"], a0)
                    for b in range(4):
                        freed[4 + b] = (took["dve"], d0)
                    swiglu(l, i)
                    state["unit"] = u0 + NE * EXPERT_UNITS

            def attention(groups, tag, qk, val, width):
                def score(n):
                    t, h = ATT[n]
                    b = next_bank("S")
                    for g in range(groups):
                        q, k = qk(h, g)
                        m = pe.matmul(psS[(b - 4) // 2][:, g * S:g * S + (t + 1) * P],
                                      q[:, t * P:(t + 1) * P], k[:, 0:(t + 1) * P], start=True, stop=True)
                    finish(m, "dve", [b, b + 1], (tag, "S", n))

                score(0)
                for n, (t, h) in enumerate(ATT):
                    if n + 1 < len(ATT):
                        score(n + 1)
                    pe.wait_ge(*from_act.more())
                    pr = PR[n % 2]
                    for kt in range(t + 1):
                        transposes("act", (tag, n, kt), [pr[:, g, kt * P:(kt + 1) * P] for g in range(groups)])
                    b = next_bank("T")
                    for kt in range(t + 1):
                        need((tag, n, kt))
                        for g in range(groups):
                            m = pe.matmul(ps[:, b, 0:64], PT[:, kt, g, :], val(kt, g, h),
                                          start=kt == 0 and g == 0, stop=kt == t and g == groups - 1)
                    finish(m, "dve", [b], (tag, "O", n))

            def fox():
                norm_T("nfox", RB)
                b = next_bank("T")
                for t in range(T):
                    for k in range(KC):
                        m = pe.matmul(ps[:, b, t * 16:(t + 1) * 16], hT[:, k, t * P:(t + 1) * P],
                                      col("foxwf", k * 16, 16), start=k == 0, stop=k == KC - 1)
                finish(m, "dve", [b], "foxF")
                pe.wait_ge(*from_dve.more())
                lf = small[:, 64:96].rearrange("p (t h) -> p t h", t=T)
                b = next_bank("T")
                pe.matmul(ps[:, b, 0:16], tri[:, :], lf[:, 0, :], start=True, stop=True)
                pe.matmul(ps[:, b, 16:32], ones[:, :], lf[:, 0, :], start=True, stop=False)
                m = pe.matmul(ps[:, b, 16:32], tri[:, :], lf[:, 1, :], start=False, stop=True)
                finish(m, "dve", [b], "foxC")
                for qd in range(QUADS):
                    for j in range(4):
                        rows_unit("act", ("fox", qd, j))
                    QA, QT = F_QA, F_QT
                    pe.wait_ge(*from_dve.more())
                    for t in range(T):
                        for g in range(2):
                            transposes("dve", ("foxT", qd, t, g), [QA[:, t, 4 * g + i, :] for i in range(4)],
                                       width=66)
                    need(("foxT", qd, T - 1, 1))
                    rows = (RA, RB)[qd % 2]
                    attention(1, ("foxP", qd), lambda h, g: (QT[0:66, h, :], QT[0:66, 4 + h, :]),
                              lambda kt, g, h: rows[:, kt, 512 + h * 64:512 + (h + 1) * 64], 64)
                project("fox2", lambda t, i: OG[:, t, i * P:(i + 1) * P])

            def dsw():
                norm_T("ndsw", RB)
                for qd in range(QUADS):
                    for j in range(3 * DG + 1):
                        rows_unit("act", ("dsw", qd, j))
                    rows = (RA, RB)[qd % 2]
                    QT = D_QT
                    pe.wait_ge(*from_dve.more())
                    for t in range(T):
                        for g in range(3):
                            transposes("act", ("dswT", qd, t, g),
                                       [rows[:, t, (4 * g + i) * P:(4 * g + i + 1) * P] for i in range(4)])
                    need(("dswT", qd, T - 1, 2))

                    def qk(h, g):
                        r = 64 * (h % 2)
                        return QT[r:r + 64, 2 * g + h // 2, :], QT[r:r + 64, 6 + 2 * g + h // 2, :]

                    attention(DG, ("dswP", qd), qk,
                              lambda kt, g, h: rows[:, kt, (6 + g) * UC + h * 64:(6 + g) * UC + (h + 1) * 64], 64)
                project("dsw2", lambda t, i: OG[:, t, i * P:(i + 1) * P])

            mixer(0)
            if want("ffn0"):
                ffn(0)
            if want("mix1"):
                mixer(1)
            if want("moe"):
                ffn(1)
            if want("fox"):
                fox()
            if want("dsw"):
                dsw()
            state["end"] = state["unit"]
            ticket["units"] = state["unit"]

        @block.sync
        def _(sp):
            sp.dma_start(colt[:, :], cols_d).then_inc(inputs_in, 16)
            sp.dma_start(rowt[:, :], rows_d.broadcast_to([P, N_ROWS])).then_inc(inputs_in, 16)
            sp.dma_start(gates_row[:, :, :].rearrange("p a b -> p (a b)"),
                         bgate_d[0:1, :].broadcast_to([P, 2 * D])).then_inc(bgate_in, 16)
            sp.dma_start(posi[:, :], pos_d).then_inc(inputs_in, 16)
            for t in range(T):
                sp.dma_start(x[:, t, :], x_d[t * P:(t + 1) * P, :]).then_inc(inputs_in, 16)
            units = ticket["units"]
            n_work = [0]
            moe = range(n_before, n_before + n_experts)

            def load(u):
                s, _, prev = plan[u]
                if prev is not None:
                    sp.wait_ge(unit_done, prev + 1)
                if s >= RING_MIX and (u - 1 < 0 or plan_kind[u] != plan_kind_prev[u]):
                    sp.wait_ge(work_free, plan_kind[u])
                sp.dma_start(ring[:, s, :], stream[u]).then_inc(landed[s], 16)

            plan_kind, plan_kind_prev = {}, {}
            for u in range(n_before + n_experts):
                in_moe = u >= n_before
                plan_kind[u] = 2 if in_moe else 1
                s, _, prev = plan[u]
                plan_kind_prev[u] = (0 if prev is None else 2 if prev >= n_before else 1)
            u = 0
            while u < min(units, n_before):
                load(u)
                u += 1
            if units > n_before:
                for k in range(RING):
                    load(n_before + k)
                with sp.Fori(0, NE - 1) as i:
                    for k in range(EXPERT_UNITS):
                        s = plan[n_before + RING + k][0]
                        sp.wait_ge(unit_done, i * EXPERT_UNITS + (n_before + k + 1))
                        sp.dma_start(ring[:, s, :],
                                     stream[bass.ds(i * EXPERT_UNITS + (n_before + RING + k), 1)]
                                     .rearrange("a p n -> (a p) n")).then_inc(landed[s], 16)
                for u in range(n_before + (NE - 1) * EXPERT_UNITS + RING, n_before + n_experts):
                    sp.wait_ge(unit_done, plan[u][2] + 1)
                    sp.dma_start(ring[:, plan[u][0], :], stream[u]).then_inc(landed[plan[u][0]], 16)
                for u in range(n_before + n_experts, units):
                    s, _, prev = plan[u]
                    sp.wait_ge(unit_done, prev + 1)
                    sp.dma_start(ring[:, s, :], stream[u]).then_inc(landed[s], 16)
            for t in range(T):
                sp.wait_ge(out_ready, 1)
                sp.dma_start(out_d[t * P:(t + 1) * P, :], x[:, t, :]).then_inc(out_written, 16)
            sp.wait_ge(out_written, 16 * T)

        @block.gpsimd
        def _(pool):
            n = [0]

            def link(ins):
                n[0] += 1
                ins.then_inc(pool_step, 1)
                pool.wait_ge(pool_step, n[0])

            link(pool.memset(ones[:, :], 1.0))
            link(pool.memset(ident[:, :], 0.0))
            link(pool.affine_select(out=ident[:, :], in_=ident[:, :], compare_op=ALU.not_equal, fill=1.0,
                                    base=0, pattern=[[-1, P]], channel_multiplier=1))
            link(pool.affine_select(out=tri[:, :], in_=ones[:, :], compare_op=ALU.is_ge, fill=0.0,
                                    base=0, pattern=[[1, P]], channel_multiplier=-1))
            link(pool.memset(causal[:, :], 0.0))
            link(pool.affine_select(out=causal[:, P:S], in_=causal[:, P:S], compare_op=ALU.is_ge, fill=NEG,
                                    base=0, pattern=[[-1, P]], channel_multiplier=1))
            link(pool.memset(causalT[:, :], 0.0))
            link(pool.affine_select(out=causalT[:, :], in_=causalT[:, :], compare_op=ALU.is_ge, fill=NEG,
                                    base=0, pattern=[[1, P]], channel_multiplier=-1))
            link(pool.memset(sel[:, :, :], 0.0))
            link(pool.affine_select(out=sel[:, :, :], in_=sel[:, :, :], compare_op=ALU.not_equal, fill=1.0,
                                    base=0, pattern=[[-1, HEADS], [0, P]], channel_multiplier=1))
            link(pool.iota(idx[:, :], pattern=[[-1, S]], base=P, channel_multiplier=1))
            link(pool.tensor_copy(dist[:, :], idx[:, :]))
            link(pool.tensor_scalar(dmask[:, 0, 0:P], dist[:, P:S], -1.0, None, ALU.mult))
            link(pool.affine_select(out=dist[:, P:S], in_=dist[:, P:S], compare_op=ALU.is_ge, fill=0.0,
                                    base=0, pattern=[[-1, P]], channel_multiplier=1))
            link(pool.affine_select(out=dmask[:, 0, 0:P], in_=dmask[:, 0, 0:P], compare_op=ALU.is_ge, fill=0.0,
                                    base=0, pattern=[[1, P]], channel_multiplier=-1))
            link(pool.tensor_tensor(dist[:, P:S], dist[:, P:S], dmask[:, 0, 0:P], ALU.add))
            link(pool.affine_select(out=dist[:, P + 64:S], in_=dist[:, P + 64:S], compare_op=ALU.is_ge,
                                    fill=-NEG, base=-64, pattern=[[0, 64]], channel_multiplier=1))
            link(pool.memset(lev[:, :, :], 0.0))
            for i, m in enumerate(LEVELS):
                v = lev[:, i, :].rearrange("p (n h m) -> p n h m", h=2, m=m)[:, :, 1, :]
                link(pool.memset(v, 1.0))
                link(pool.affine_select(out=v, in_=v, compare_op=ALU.is_ge, fill=0.0, base=0,
                                        pattern=[[-2 * m, P // (2 * m)], [0, m]], channel_multiplier=1))
                link(pool.affine_select(out=v, in_=v, compare_op=ALU.is_ge, fill=0.0, base=m - 1,
                                        pattern=[[2 * m, P // (2 * m)], [0, m]], channel_multiplier=-1))
            pool.memset(junk[:, :], 0.0).then_inc(masks_made, 1)


        @block.scalar
        def _(act):
            step, took = Count(act_step), Count(act_took)
            gave_pe, gave_dve = Count(act_gave_pe), Count(act_gave_dve)
            from_dve = Count(dve_gave_act)

            def link(ins, c=step):
                ins.then_inc(c.sem, 1)
                act.wait_ge(*c.more())

            def fn(out, in_, func, **kw):
                return nc.scalar.activation(out, in_, func, **kw)

            def taken(key):
                who, n = ticket[key]
                act.wait_ge({"dve": dve_took, "act": act_took}[who], n)

            def rows_out(key, dst, func=ACT.Copy, turn=None):
                b = bank_of(act, key, turn)
                link(fn(dst, ps[:, b, :].rearrange("p (t c) -> p t c", t=T), func), took)

            def blocks_out(key, dst, n=4, turn=None):
                b = bank_of(act, key, turn)
                link(fn(dst, ps[:, b, 0:n * P].rearrange("p (n s) -> p n s", n=n), ACT.Copy), took)

            def root(a):
                act.wait_ge(*from_dve.more())
                link(fn(a, a, ACT.Sqrt), gave_dve)

            def norm_T(first=False):
                if not first:
                    act.wait_ge(*from_dve.more())
                for t in range(T):
                    link(fn(RB[:, t, 0:D], x[:, t, :], ACT.Square, accum_out=ssx[:, t:t + 1]), gave_dve)
                root(ssx)

            def softplus_of_minus_abs(dst, src, c):
                link(fn(dst, src, ACT.Abs))
                link(fn(dst, dst, ACT.Exp, scale=-1.0))
                link(fn(dst, dst, ACT.Ln, bias=1.0), c)

            def setup():
                act.wait_ge(inputs_in, 16 * 5)
                link(fn(cond[:, :], col("c", 0, KC), ACT.Silu), gave_dve)
                act.wait_ge(*from_dve.more())
                link(fn(lamt[:, 0:4], small[:, 0:4], ACT.Exp), gave_dve)
                act.wait_ge(*from_dve.more())
                link(fn(lbc[:, 2, :], lbc[:, 3, :], ACT.Sigmoid, scale=-1.0))
                softplus_of_minus_abs(lbc[:, 4, :], lbc[:, 3, :], gave_dve)
                act.wait_ge(*from_dve.more())
                link(fn(sinr[:, :, :], sinr[:, :, :], ACT.Sin))
                link(fn(cosr[:, :, :], cosr[:, :, :], ACT.Sin), gave_dve)

            def diff_attention(l):
                root(meansq[:, 0:32])
                for t in range(T):
                    nk = (t + 1) * P
                    for h in range(HEADS):
                        act.wait_ge(*from_dve.more())
                        link(fn(A_E[:, 0:nk], A_S[:, 0:nk], ACT.Exp, bias=negS[:, 0:1],
                                accum_out=sumS[:, 0:1]))
                        link(fn(A_E[:, nk:2 * nk], A_S[:, nk:2 * nk], ACT.Exp, bias=negS[:, 1:2],
                                accum_out=sumS[:, 1:2]), gave_dve)
                        blocks_out(("aA", l, t, h), aT_sb[:, 0:t + 1, :], t + 1)
                root(meansq[:, 0:8])

            def hgrn(l):
                for i, dst in enumerate((B_B, B_Q)):
                    for t in range(T):
                        blocks_out(("bT", l, i, t), dst[:, :, t * P:(t + 1) * P])
                link(fn(B_K, B_B, ACT.Sigmoid, scale=-1.0))
                softplus_of_minus_abs(B_E, B_B, gave_dve)
                if l > 0:
                    act.wait_ge(*from_dve.more())
                    softplus_of_minus_abs(B_QP, B_QP, gave_dve)
                for _ in LEVELS:
                    act.wait_ge(*from_dve.more())
                    link(fn(B_E, B_E, ACT.Abs))
                    link(fn(B_E, B_E, ACT.Exp, scale=-1.0), gave_dve)
                act.wait_ge(*from_dve.more())
                for h in range(HEADS):
                    link(fn(B_E[:, h, 0:P], B_B[:, h, 0:P], ACT.Exp, scale=-1.0, bias=B_B[:, h, P - 1:P]))
                link(fn(B_E[:, :, P:S], B_B[:, :, P:S], ACT.Exp), gave_dve)
                root(meansq[:, 0:8])

            def mlstm(l):
                for t in range(T):
                    for g in range(2):
                        blocks_out(("cT", l, t, g), C_PAD[:, 4 * g:4 * g + 4, 3 + t * P:3 + (t + 1) * P])
                taken(("cG", l))
                softplus_of_minus_abs(C_B4, C_F4, gave_dve)
                act.wait_ge(*from_dve.more())
                link(fn(C_EM4, C_EM4, ACT.Exp, scale=-1.0), gave_pe)
                act.wait_ge(*from_dve.more())
                link(fn(C_QK, C_QK, ACT.Silu), gave_pe)
                for h in range(HEADS):
                    act.wait_ge(*from_dve.more())
                    link(fn(C_E[:, 0:S], C_G[:, 0:S], ACT.Exp, bias=small[:, 256 + h:257 + h]))
                    link(fn(C_E[:, S:S + P], C_G[:, S:S + P], ACT.Exp, bias=small[:, 260 + h:261 + h]), gave_dve)
                root(meansq[:, 0:8])

            def project(tag):
                for t in range(T):
                    for g in range(2):
                        blocks_out((tag, t, g), hT[:, 4 * g:4 * g + 4, t * P:(t + 1) * P])

            def mixer(l):
                norm_T(first=l == 0)
                for j in range(6):
                    rows_out(("a", l, j), RA[:, :, j * UC:(j + 1) * UC])
                for j in range(8):
                    rows_out(("b", l, j), RB[:, :, j * UC:(j + 1) * UC],
                             ACT.Silu if j in (2, 3, 6, 7) else ACT.Copy)
                diff_attention(l)
                for j in range(4):
                    rows_out(("c", l, j), RA[:, :, j * UC:(j + 1) * UC])
                for j in range(2):
                    b = bank_of(act, ("c", l, 4 + j))
                    for t in range(T):
                        o = 1024 + 2 * j * CV
                        ins = fn(RA[:, t, o:o + 2 * CV].rearrange("p (h c) -> p h c", h=2)[:, :, 0:HD],
                                 ps[:, b, t * UC:(t + 1) * UC].rearrange("p (h c) -> p h c", h=2), ACT.Copy)
                        link(ins, took if t else step)
                for j in range(2):
                    rows_out(("c", l, 6 + j), RA[:, :, 1540 + j * UC:1540 + (j + 1) * UC], ACT.Sigmoid)
                hgrn(l)
                mlstm(l)
                for br in range(3):
                    if br == 2:
                        taken(("branch", l, 0, 1))
                    for j in range(4):
                        o = (br % 2) * D + j * UC
                        rows_out(("gate", l, br, j), RB[:, :, o:o + UC], ACT.Sigmoid)
                project(f"m{l}")

            def swiglu(l, turn=None):
                def turned(g):
                    blocks_out(("act", l, g), actT[:, g % 2, :, :].rearrange("p k (t s) -> p (k t) s", t=T),
                               4, turn)

                for g in range(FG):
                    rows_out(("w1", l, g), gate_h[:, g % 2, :].rearrange("p (t c) -> p t c", t=T), ACT.Silu, turn)
                    if g >= 1:
                        turned(g - 1)
                turned(FG - 1)

            def ffn(l):
                norm_T()
                if l == 0:
                    swiglu(l)
                    return
                act.wait_ge(*from_dve.more())
                link(fn(comb[:, :, :], comb[:, :, :], ACT.Exp), gave_dve)
                with turns(act, NE, {took: 2 * FG}) as i:
                    swiglu(l, i)

            def attention(groups, tag):
                def exps(n):
                    t, _ = ATT[n]
                    act.wait_ge(*from_dve.more())
                    link(fn(PR[n % 2][:, 0:groups, 0:(t + 1) * P], D_S[n % 2][:, 0:groups, 0:(t + 1) * P],
                            ACT.Exp, bias=negS[:, n:n + 1], accum_out=sumS[:, n:n + 1]), gave_pe)

                exps(0)
                for n, (t, _) in enumerate(ATT):
                    if n + 1 < len(ATT):
                        exps(n + 1)
                    for kt in range(t + 1):
                        blocks_out((tag, n, kt), PT[:, kt, 0:groups, :], groups)

            def fox():
                norm_T()
                taken("foxF")
                softplus_of_minus_abs(small[:, 64:96], small[:, 32:64], gave_dve)
                for qd in range(QUADS):
                    rows = (RA, RB)[qd % 2]
                    for j in range(4):
                        rows_out(("fox", qd, j), rows[:, :, j * UC:(j + 1) * UC], ACT.Silu if j == 3 else ACT.Copy)
                    root(meansq[:, 0:16])
                    attention(1, ("foxP", qd))
                project("fox2")

            def dsw():
                norm_T()
                for qd in range(QUADS):
                    rows = (RA, RB)[qd % 2]
                    for j in range(3 * DG + 1):
                        rows_out(("dsw", qd, j), rows[:, :, j * UC:(j + 1) * UC],
                                 ACT.Silu if j == 3 * DG else ACT.Copy)
                    root(meansq[:, 0:48])
                    for t in range(T):
                        for g in range(3):
                            blocks_out(("dswT", qd, t, g), D_QT[:, 4 * g:4 * g + 4, t * P:(t + 1) * P])
                    attention(DG, ("dswP", qd))
                project("dsw2")

            setup()
            mixer(0)
            if want("ffn0"):
                ffn(0)
            if want("mix1"):
                act.wait_ge(gates_free, 1)
                act.dma_start(gates_row[:, :, :].rearrange("p a b -> p (a b)"),
                              bgate_d[1:2, :].broadcast_to([P, 2 * D])).then_inc(bgate_in, 16)
                mixer(1)
            if want("moe"):
                ffn(1)
            if want("fox"):
                fox()
            if want("dsw"):
                dsw()

        @block.vector
        def _(dve):
            step, took = Count(dve_step), Count(dve_took)
            gave_pe, gave_act = Count(dve_gave_pe), Count(dve_gave_act)
            from_act = Count(act_gave_dve)
            v = nc.vector

            def link(ins, c=step):
                ins.then_inc(c.sem, 1)
                dve.wait_ge(*c.more())

            def taken(key, turn=None):
                _, n = ticket[key]
                dve.wait_ge(act_took, n if turn is None else turn * (2 * FG) + n)

            def tt(out, a, b, op, c=step):
                link(v.tensor_tensor(out, a, b, op), c)

            def ts(out, a, s1, s2, op0, op1=None, c=step):
                if op1 is None:
                    link(v.tensor_scalar(out, a, s1, None, op0), c)
                else:
                    link(v.tensor_scalar(out, a, s1, s2, op0, op1), c)

            def stt(out, a, s_, b, op0, op1, c=step):
                link(v.scalar_tensor_tensor(out, a, s_, b, op0, op1), c)

            def view(b, n, w=P):
                return ps[:, b, 0:n * w].rearrange("p (n s) -> p n s", n=n)

            def inverse_root(a, n):
                ts(a, a, 1.0 / n, EPS, ALU.mult, ALU.add, c=gave_act)
                dve.wait_ge(*from_act.more())
                link(v.reciprocal(a, a))

            def square_sums(out, src, sq, n, w):
                tt(sq, src, src, ALU.mult)
                link(v.tensor_reduce(out, sq.rearrange("p (n w) -> p n w", n=n), X, ALU.add))

            def norm_T(tag, scale, shift):
                for t in range(T):
                    dve.wait_ge(*from_act.more())
                inverse_root(ssx, D)
                for t in range(T):
                    ts(RB[:, t, 0:D], x[:, t, :], ssx[:, t:t + 1], None, ALU.mult, c=gave_pe)
                for t in range(T):
                    for g in range(2):
                        b = bank_of(dve, (tag, t, g))
                        for i in range(4):
                            k = 4 * g + i
                            o, src = hT[:, k, t * P:(t + 1) * P], ps[:, b, i * P:(i + 1) * P]
                            c = took if i == 3 else step
                            if shift is None:
                                ts(o, src, scale[:, k:k + 1], None, ALU.mult, c=c)
                            else:
                                ts(o, src, scale[:, k:k + 1], shift[:, k:k + 1], ALU.mult, ALU.add, c=c)

            def setup():
                dve.wait_ge(inputs_in, 16 * 5)
                dve.wait_ge(masks_made, 1)
                lamr = row("lam").rearrange("p (l i d) -> p l i d", l=DEPTH, i=4)
                for l in range(DEPTH):
                    for i in range(2):
                        c = gave_act if l == DEPTH - 1 and i == 1 else step
                        link(v.scalar_tensor_tensor(junk[:, 0:AK], lamr[:, l, 2 * i, :], 1.0, lamr[:, l, 2 * i + 1, :],
                                                    ALU.mult, ALU.mult, accum_out=small[:, 2 * l + i:2 * l + i + 1]), c)
                dve.wait_ge(*from_act.more())
                dve.wait_ge(*from_act.more())
                for l in range(DEPTH):
                    lam_init = 0.8 - 0.6 * math.exp(-0.3 * l)
                    tt(lamt[:, 4 + l:5 + l], lamt[:, 2 * l + 1:2 * l + 2], lamt[:, 2 * l:2 * l + 1], ALU.subtract)
                    ts(lamt[:, 4 + l:5 + l], lamt[:, 4 + l:5 + l], -lam_init, None, ALU.add)
                d, m0 = lbc[:, 3, :], lbc[:, 5, :]
                tt(d, col("lb", HEADS, HEADS), col("lb", 0, HEADS), ALU.subtract, c=gave_act)
                dve.wait_ge(*from_act.more())
                ts(m0, d, 0.0, None, ALU.min)
                tt(lbc[:, 0, :], m0, lbc[:, 4, :], ALU.subtract)
                tt(lbc[:, 1, :], lbc[:, 0, :], d, ALU.subtract)
                for g, r in enumerate(DILATIONS):
                    link(v.tensor_scalar(idx2[:, :], idx[:, :], r - 1, None, ALU.bitwise_and))
                    ts(dmask[:, g, :], idx2[:, :], 0.0, NEG, ALU.is_gt, ALU.mult)
                    tt(dmask[:, g, :], dmask[:, g, :], causal[:, :], ALU.add)
                tt(dmask[:, 0, 0:P], dmask[:, 0, 0:P], causalT[:, :], ALU.add)
                link(v.memset(qc66[:, :], 1.0))
                ts(qc66[0:64, 0:1], col("foxq")[0:64, :], 0.125, None, ALU.mult)
                link(v.tensor_copy(qc66[0:64, 1:2], col("foxk")[0:64, :]))
                inv = (np.float32(500000.0) ** (-np.arange(0, 16, 2, dtype=np.float32) / np.float32(16)))
                posf, turns_ = small[:, 16:18], cosr[:, :, :]
                link(v.tensor_copy(posf, posi[:, :]))
                for j in range(ROT):
                    ts(sinr[:, :, j:j + 1], posf.unsqueeze(2), float(inv[j]), None, ALU.mult)
                two_pi = 2 * math.pi
                c1 = 6.28125
                c2 = float(np.float32(int((two_pi - c1) * 2 ** 20) / 2 ** 20))
                c3 = two_pi - c1 - c2
                ts(turns_, sinr[:, :, :], 1 / two_pi, None, ALU.mult)
                ts(turns_, turns_, 12582912.0, None, ALU.add)
                ts(turns_, turns_, -12582912.0, None, ALU.add)
                for c_ in (c1, c2, c3):
                    stt(sinr[:, :, :], turns_, -c_, sinr[:, :, :], ALU.mult, ALU.add)
                ts(cosr[:, :, :], sinr[:, :, :], math.pi / 2, None, ALU.add)
                w = small[:, 20:36].rearrange("p (t j) -> p t j", t=T)
                ts(w, cosr[:, :, :], math.pi, -two_pi, ALU.is_gt, ALU.mult)
                tt(cosr[:, :, :], cosr[:, :, :], w, ALU.add)
                ts(cosr[:, :, :], cosr[:, :, :], 3.1415925, -3.1415925, ALU.min, ALU.max)
                ts(sinr[:, :, :], sinr[:, :, :], 3.1415925, -3.1415925, ALU.min, ALU.max, c=gave_act)
                dve.wait_ge(*from_act.more())

            def mod(l):
                cb = RA[:, 0, 0:KC * P].rearrange("p (k n) -> p k n", k=KC)
                link(v.tensor_copy(cb, cond[:, :].unsqueeze(2).broadcast_to([P, KC, P])), gave_pe)
                dve.wait_ge(bgate_in, 16 * (l + 1))
                for j in range(24):
                    b = bank_of(dve, ("mod", l, j))
                    part = j // 4
                    if part in (2, 5):
                        o = gates_row[:, part // 3, (j % 4) * UC:(j % 4 + 1) * UC]
                        tt(o, ps[:, b, 0:UC], o, ALU.add, c=took)
                    else:
                        for i in range(2):
                            k = 2 * j + i
                            link(v.scalar_tensor_tensor(junk[:, :], ps[:, b, i * P:(i + 1) * P], 1.0, ident[:, :],
                                                        ALU.mult, ALU.mult, accum_out=modc[:, k:k + 1]),
                                 took if i else step)
                for lo in (0, 24):
                    tt(modc[:, lo:lo + 16], modc[:, lo:lo + 16], col("bmod", l * 48 + lo, 16), ALU.add)
                stt(A1[:, :], modc[:, 8:16], 1.0, col("n1", l * KC, KC), ALU.add, ALU.mult)
                stt(A2[:, :], modc[:, 32:40], 1.0, col("n2", l * KC, KC), ALU.add, ALU.mult)

            def head_norm(Y, sq, gate=None):
                for t in range(T):
                    square_sums(meansq[:, 4 * t:4 * t + 4], Y[:, t, :, :].rearrange("p h d -> p (h d)"),
                                sq[:, 0:512], HEADS, HD)
                inverse_root(meansq[:, 0:8], HD)
                for t in range(T):
                    r = meansq[:, 4 * t:4 * t + 4].unsqueeze(2).broadcast_to([P, HEADS, HD])
                    tt(Y[:, t, :, :], Y[:, t, :, :], r, ALU.mult, c=step if gate else gave_pe)
                    if gate:
                        y = Y[:, t, :, :].rearrange("p h d -> p (h d)")
                        tt(y, y, gate(t), ALU.mult, c=gave_pe)

            def y_T(l, br, w, factor=1.0):
                for t in range(T):
                    b = bank_of(dve, ("yT", l, br, t))
                    ts(YT[:, br, :, t * P:(t + 1) * P], view(b, 4), w, factor, ALU.mult, ALU.mult, c=took)

            def diff_attention(l):
                lam_init = 0.8 - 0.6 * math.exp(-0.3 * l)
                taken(("a", l, 5))
                for t in range(T):
                    square_sums(meansq[:, 16 * t:16 * t + 16], RA[:, t, 0:1024], A_SQ, 16, AK)
                inverse_root(meansq[:, 0:32], AK)
                for t in range(T):
                    r = RA[:, t, 0:1024].rearrange("p (n d) -> p n d", n=16)
                    tt(r, r, meansq[:, 16 * t:16 * t + 16].unsqueeze(2).broadcast_to([P, 16, AK]), ALU.mult,
                       c=gave_pe)
                for t in range(T):
                    for g in range(2):
                        b = bank_of(dve, ("aT", l, t, g))
                        ts(A_QT[:, 4 * g:4 * g + 4, t * P:(t + 1) * P], view(b, 4),
                           col(("aq", "ak")[g], l), (AK ** -0.5, 1.0)[g], ALU.mult, ALU.mult, c=took)
                for t in range(T):
                    nk = (t + 1) * P
                    for h in range(HEADS):
                        b = bank_of(dve, ("aS", l, t, h))
                        d = dist[:, S - nk:S].unsqueeze(1).broadcast_to([P, 2, nk])
                        sc = A_S[:, 0:2 * nk].rearrange("p (m k) -> p m k", m=2)
                        stt(sc, d, -SLOPES[h], view(b, 2, nk), ALU.mult, ALU.add, c=took)
                        link(v.tensor_reduce(negS[:, 0:2], sc, X, ALU.max, negate=True), gave_act)
                        dve.wait_ge(*from_act.more())
                        link(v.reciprocal(recS[:, 0:2], sumS[:, 0:2]))
                        tt(recS[:, 1:2], recS[:, 1:2], lamt[:, 4 + l:5 + l], ALU.mult)
                        a = A_W[:, h % 2, 0:nk]
                        ts(a, A_E[:, 0:nk], recS[:, 0:1], None, ALU.mult)
                        stt(a, A_E[:, nk:2 * nk], recS[:, 1:2], a, ALU.mult, ALU.add, c=gave_pe)
                    b = bank_of(dve, ("aO", l, t))
                    link(v.tensor_copy(Y_A[:, t, :, :], view(b, HEADS)), took)
                head_norm(Y_A, A_SQ)
                y_T(l, 0, col("subln", l), 1.0 - lam_init)

            def hgrn(l):
                dve.wait_ge(*from_act.more())
                stt(B_E, B_B, 0.0, B_E, ALU.min, ALU.subtract)
                if l > 0:
                    for h in range(HEADS):
                        ts(B_QP[:, h, :], B_E[:, h, :], lbc[:, 3, h:h + 1], None, ALU.subtract)
                        ts(B_KP[:, h, :], B_E[:, h, :], lbc[:, 1, h:h + 1], lbc[:, 0, h:h + 1], ALU.add, ALU.max,
                           c=gave_act if h == HEADS - 1 else step)
                    for h in range(HEADS):
                        ts(B_K[:, h, :], B_K[:, h, :], lbc[:, 2, h:h + 1], None, ALU.mult)
                    dve.wait_ge(*from_act.more())
                    tt(B_E, B_KP, B_QP, ALU.add)
                for h in range(HEADS):
                    for t in range(T):
                        o, s_ = B_B[:, h, t * P:(t + 1) * P], B_E[:, h, t * P:(t + 1) * P]
                        link(v.tensor_tensor_scan(o, ones[:, :], s_, 0.0, ALU.mult, ALU.add),
                             gave_pe if h == HEADS - 1 and t else step)
                flat = lambda a: a.rearrange("p h s -> p (h s)")

                def to_middle(m):
                    n = HEADS * S // (2 * m)
                    bb = flat(B_B).rearrange("p (n w) -> p n w", n=n)
                    e = flat(B_E).rearrange("p (n w) -> p n w", n=n)
                    tt(e, bb, bb[:, :, m - 1:m].broadcast_to([P, n, 2 * m]), ALU.subtract, c=gave_act)

                to_middle(LEVELS[0])
                for t in range(T):
                    b = bank_of(dve, ("lev", l, 0, t))
                    tt(B_ATT[:, t, :, :], view(b, 4), ident[:, :].unsqueeze(1).broadcast_to([P, 4, P]), ALU.mult,
                       c=took)
                for i, m in enumerate(LEVELS):
                    dve.wait_ge(*from_act.more())
                    tt(B_QP, B_Q, B_E, ALU.mult)
                    tt(B_KP, B_K, B_E, ALU.mult, c=gave_pe)
                    if i + 1 < len(LEVELS):
                        to_middle(LEVELS[i + 1])
                    for t in range(T):
                        b = bank_of(dve, ("lev", l, i + 1, t))
                        tmp = B_TMP.rearrange("p (h s) -> p h s", h=HEADS)
                        tt(tmp, view(b, 4), lev[:, i, :].unsqueeze(1).broadcast_to([P, 4, P]), ALU.mult, c=took)
                        tt(B_ATT[:, t, :, :], B_ATT[:, t, :, :], tmp, ALU.add,
                           c=gave_act if i == len(LEVELS) - 1 and t else step)
                dve.wait_ge(*from_act.more())
                tt(B_QP[:, :, P:S], B_Q[:, :, P:S], B_E[:, :, P:S], ALU.mult)
                tt(B_KP[:, :, 0:P], B_K[:, :, 0:P], B_E[:, :, 0:P], ALU.mult, c=gave_pe)
                b = bank_of(dve, ("levx", l))
                link(v.tensor_copy(B_ATTX, view(b, 4)), took)
                for t in range(T):
                    b = bank_of(dve, ("bO", l, t))
                    link(v.tensor_copy(Y_B[:, t, :, :], view(b, HEADS)), took)
                head_norm(Y_B, B_TMP, lambda t: RB[:, t, 1536:2048])
                y_T(l, 1, col("gnorm", l))

            def mlstm(l):
                link(v.memset(C_PAD[:, :, 0:3], 0.0))
                link(v.memset(RA[:, :, 1024:1024 + HEADS * CV].rearrange("p t (h c) -> p t h c", h=HEADS)
                              [:, :, :, HD:CV], 1.0))
                b = bank_of(dve, ("cG", l))
                ts(C_I4, ps[0:4, b, 0:S], col("ib", l)[0:4, :], None, ALU.add)
                ts(C_F4, ps[0:4, b, S:2 * S], col("fb", l)[0:4, :], None, ALU.add, c=took)
                dve.wait_ge(*from_act.more())
                stt(C_B4, C_F4, 0.0, C_B4, ALU.min, ALU.subtract)
                link(v.tensor_tensor_scan(C_F4[:, 0:P], ones[0:4, :], C_B4[:, 0:P], 0.0, ALU.mult, ALU.add))
                link(v.tensor_tensor_scan(C_F4[:, P:S], ones[0:4, :], C_B4[:, P:S], C_F4[:, P - 1:P],
                                          ALU.mult, ALU.add))
                tt(C_R4, C_I4, C_F4, ALU.subtract)
                link(v.tensor_tensor_scan(C_M4, C_R4, C_R4, 0.0, ALU.max, ALU.max))
                tt(C_EM4, C_F4, C_M4, ALU.add, c=gave_act)
                taken(("cT", l, 1, 1))
                for k in range(8):
                    w = lambda j: col("convw", l * 32 + k * 4 + j)
                    ts(C_QK[:, k, :], C_PAD[:, k, 0:S], w(0), col("convb", l * 8 + k), ALU.mult, ALU.add)
                    for j in range(1, 4):
                        stt(C_QK[:, k, :], C_PAD[:, k, j:j + S], w(j), C_QK[:, k, :], ALU.mult, ALU.add,
                            c=gave_act if k == 7 and j == 3 else step)
                b = bank_of(dve, ("cR", l))
                link(v.tensor_copy(small[:, 256:272], ps[:, b, 0:16]), took)
                for hp in range(2):
                    b = bank_of(dve, ("cM", l, hp))
                    link(v.tensor_copy(C_M[:, 2 * hp:2 * hp + 2, :], view(b, 2, S)), took)
                for h in range(HEADS):
                    stt(C_G[:, 0:P], C_M[:, h, 0:P], -1.0, causalT[:, :], ALU.mult, ALU.add)
                    ts(C_G[:, P:S], C_M[:, h, P:S], -1.0, None, ALU.mult)
                    stt(C_G[:, S:S + P], C_M[:, h, P:S], -1.0, causalT[:, :], ALU.mult, ALU.add, c=gave_act)
                    dve.wait_ge(*from_act.more())
                    b = bank_of(dve, ("cw", l, h))
                    stt(C_W, ps[:, b, 0:384], HD ** -0.5, C_E, ALU.mult, ALU.mult, c=took)
                    b = bank_of(dve, ("cO", l, h))
                    o = ps[:, b, :].rearrange("p (t c) -> p t c", t=T)
                    den = small[:, 272:274]
                    em = small[:, 264:272].rearrange("p (t h) -> p t h", t=T)
                    ts(den.unsqueeze(2), o[:, :, HD:CV], -1.0, None, ALU.mult)
                    tt(den.unsqueeze(2), den.unsqueeze(2), o[:, :, HD:CV], ALU.max)
                    tt(den.unsqueeze(2), den.unsqueeze(2), em[:, :, h:h + 1], ALU.max)
                    link(v.reciprocal(den, den))
                    for t in range(T):
                        ts(Y_C[:, t, h, :], o[:, t, 0:HD], den[:, t:t + 1], None, ALU.mult,
                           c=took if t else step)
                head_norm(Y_C, C_QK.rearrange("p b s -> p (b s)"), lambda t: RA[:, t, 1540:2052])
                y_T(l, 2, col("cnorm", l))

            def merge(l, br):
                tmp = W[:, 0:1024].rearrange("p (t c) -> p t c", t=T)
                taken(("gate", l, br, 3))
                for j in range(2):
                    b = bank_of(dve, ("branch", l, br, j))
                    o = (br % 2) * D + j * 512
                    out = RA[:, :, j * 512:(j + 1) * 512]
                    dst = out if br == 0 else tmp
                    tt(dst, ps[:, b:b + 2, :], RB[:, :, o:o + 512], ALU.mult, c=took)
                    if br == 0:
                        continue
                    if br == 2 and j == 1:
                        for t in range(T):
                            tt(out[:, t, :], out[:, t, :], tmp[:, t, :], ALU.add, c=gave_pe)
                    else:
                        tt(out, out, tmp, ALU.add)

            def add_rows(tag, gate=None):
                tmp = RB[:, :, 2048:2304]
                for j in range(4):
                    b = bank_of(dve, (tag, j))
                    if gate is None:
                        link(v.tensor_copy(tmp, view(b, T, UC)), took)
                    else:
                        g = gate[:, j * UC:(j + 1) * UC].unsqueeze(1).broadcast_to([P, T, UC])
                        tt(tmp, view(b, T, UC), g, ALU.mult, c=took)
                    o = x[:, :, j * UC:(j + 1) * UC]
                    tt(o, o, tmp, ALU.add, c=gave_act if j == 3 else step)

            def mixer(l):
                mod(l)
                norm_T(f"n1{l}", A1, modc[:, 0:8])
                diff_attention(l)
                hgrn(l)
                mlstm(l)
                for br in range(3):
                    merge(l, br)
                v.memset(junk[:, 0:1], 0.0).then_inc(work_free, 1)
                add_rows(f"m{l}o", gates_row[:, 0, :])

            def hidden(l, turn=None):
                for g in range(FG):
                    taken(("w1", l, g), turn)
                    b = bank_of(dve, ("w3", l, g), turn)
                    tt(hid[:, g % 2, :, :], view(b, T, UC),
                       gate_h[:, g % 2, :].rearrange("p (t c) -> p t c", t=T), ALU.mult, c=took)

            def ffn(l):
                norm_T(f"n2{l}", A2, modc[:, 24:32])
                if l == 0:
                    hidden(l)
                    bank_of(dve, ("y", l))
                    for t in range(T):
                        y = ps[:, 4 + 2 * t:6 + 2 * t, :].rearrange("p a b -> p (a b)")
                        tt(RB[:, t, 0:D], y, gates_row[:, 1, :], ALU.mult, c=took)
                        if t == T - 1:
                            v.memset(junk[:, 0:1], 0.0).then_inc(gates_free, 1)
                        tt(x[:, t, :], x[:, t, :], RB[:, t, 0:D], ALU.add, c=gave_act if t else step)
                    return
                b = bank_of(dve, "router")
                lg = ps[:, b, 0:T * NE].rearrange("p (t e) -> p t e", t=T)
                tt(comb[:, :, :], lg, row("rb").unsqueeze(1).broadcast_to([P, T, NE]), ALU.add, c=took)
                mx = small[:, 216:218]
                link(v.tensor_reduce(mx, comb[:, :, :], X, ALU.max))
                tt(comb[:, :, :], comb[:, :, :], mx.unsqueeze(2).broadcast_to([P, T, NE]), ALU.subtract, c=gave_act)
                cnt = small[:, 220:236].rearrange("p (t e) -> p t e", t=T)
                link(v.memset(cnt, 0.0))
                link(v.memset(moe_sum, 0.0))
                dve.wait_ge(*from_act.more())
                for t in range(T):
                    for e in range(NE):
                        me = comb[:, t, e:e + 1]
                        stt(cnt[:, t, :], comb[:, t, :], me, cnt[:, t, :], ALU.is_lt, ALU.add)
                        if e + 1 < NE:
                            stt(cnt[:, t, e + 1:NE], comb[:, t, e + 1:NE], me, cnt[:, t, e + 1:NE],
                                ALU.is_equal, ALU.add)
                stt(comb[:, :, :], cnt, float(2), comb[:, :, :], ALU.is_lt, ALU.mult)
                link(v.tensor_reduce(mx, comb[:, :, :], X, ALU.add))
                link(v.reciprocal(mx, mx))
                tt(comb[:, :, :], comb[:, :, :], mx.unsqueeze(2).broadcast_to([P, T, NE]), ALU.mult)
                with turns(dve, NE, {took: FG + T, step: 2}) as i:
                    hidden(l, i)
                    bank_of(dve, ("y", l), i)
                    for t in range(T):
                        y = ps[:, 4 + 2 * t:6 + 2 * t, :].rearrange("p a b -> p (a b)")
                        stt(moe_sum[:, t, :], y, comb[:, t, 0:1], moe_sum[:, t, :], ALU.mult, ALU.add, c=took)
                    nxt = cnt[:, :, 0:NE - 1]
                    link(v.tensor_copy(nxt, comb[:, :, 1:NE]))
                    link(v.tensor_copy(comb[:, :, 0:NE - 1], nxt))
                for t in range(T):
                    tt(RB[:, t, 0:D], moe_sum[:, t, :], gates_row[:, 1, :], ALU.mult)
                    tt(x[:, t, :], x[:, t, :], RB[:, t, 0:D], ALU.add, c=gave_act if t else step)

            def attention(groups, tag, mask, scale, qd, rows, gate_at):
                def score(n):
                    t, h = ATT[n]
                    nk = (t + 1) * P
                    b = bank_of(dve, (tag, "S", n))
                    src = psS[(b - 4) // 2][:, 0:groups * S].rearrange("p (g k) -> p g k", g=groups)[:, :, 0:nk]
                    d = D_S[n % 2][:, 0:groups, 0:nk]
                    stt(d, src, scale, mask[:, :, S - nk:S], ALU.mult, ALU.add, c=took)
                    link(v.tensor_reduce(negS[:, n:n + 1], d, mybir.AxisListType.XY, ALU.max, negate=True), gave_act)

                score(0)
                for n, (t, h) in enumerate(ATT):
                    if n + 1 < len(ATT):
                        score(n + 1)
                    b = bank_of(dve, (tag, "O", n))
                    link(v.reciprocal(recS[:, n:n + 1], sumS[:, n:n + 1]))
                    o = qd * UC + h * 64
                    ts(OG[:, t, o:o + 64], ps[:, b, 0:64], recS[:, n:n + 1], None, ALU.mult, c=took)
                for t in range(T):
                    o = OG[:, t, qd * UC:(qd + 1) * UC]
                    tt(o, o, rows[:, t, gate_at:gate_at + UC], ALU.mult, c=gave_pe if qd == QUADS - 1 else step)

            def fox():
                norm_T("nfox", col("ng", 0, KC), None)
                b = bank_of(dve, "foxF")
                f = small[:, 32:64].rearrange("p (t h) -> p t h", t=T)
                tt(f, ps[:, b, 0:32].rearrange("p (t h) -> p t h", t=T),
                   row("foxbf").unsqueeze(1).broadcast_to([P, T, 16]), ALU.add, c=took)
                dve.wait_ge(*from_act.more())
                stt(small[:, 64:96], small[:, 32:64], 0.0, small[:, 64:96], ALU.min, ALU.subtract, c=gave_pe)
                b = bank_of(dve, "foxC")
                link(v.tensor_copy(small[:, 96:128], ps[:, b, 0:32]), took)
                c = small[:, 96:128].rearrange("p (t h) -> p t h", t=T)
                link(v.memset(F_QA[:, :, 0:4, 65:66], 1.0))
                link(v.memset(F_QA[:, :, 4:8, 64:65], 1.0))
                for qd in range(QUADS):
                    rows = (RA, RB)[qd % 2]
                    taken(("fox", qd, 3))
                    for t in range(T):
                        square_sums(meansq[:, 8 * t:8 * t + 8], rows[:, t, 0:512], D_SQ[:, 0:512], 8, 64)
                    inverse_root(meansq[:, 0:16], 64)
                    for t in range(T):
                        r = meansq[:, 8 * t:8 * t + 8].unsqueeze(2).broadcast_to([P, 8, 64])
                        tt(F_QA[:, t, :, 0:64], rows[:, t, 0:512].rearrange("p (v d) -> p v d", v=8), r, ALU.mult)
                    cq = c[:, :, 4 * qd:4 * qd + 4].unsqueeze(3)
                    link(v.tensor_copy(F_QA[:, :, 0:4, 64:65], cq))
                    ts(F_QA[:, :, 4:8, 65:66], cq, -1.0, None, ALU.mult, c=gave_pe)
                    for t in range(T):
                        for g in range(2):
                            b = bank_of(dve, ("foxT", qd, t, g))
                            ts(F_QT[0:66, 4 * g:4 * g + 4, t * P:(t + 1) * P],
                               ps[0:66, b, :].rearrange("p (n s) -> p n s", n=4), qc66[0:66, g:g + 1], None,
                               ALU.mult, c=took)
                    attention(1, ("foxP", qd), causal[:, :].unsqueeze(1), 1.0, qd, rows, 3 * UC)
                add_rows("fox2o")

            def dsw():
                norm_T("ndsw", col("ng", KC, KC), None)
                for qd in range(QUADS):
                    rows = (RA, RB)[qd % 2]
                    taken(("dsw", qd, 3 * DG))
                    for t in range(T):
                        square_sums(meansq[:, 24 * t:24 * t + 24], rows[:, t, 0:1536], D_SQ, 24, 64)
                    inverse_root(meansq[:, 0:48], 64)
                    for t in range(T):
                        r = rows[:, t, 0:1536].rearrange("p (n d) -> p n d", n=24)
                        tt(r, r, meansq[:, 24 * t:24 * t + 24].unsqueeze(2).broadcast_to([P, 24, 64]), ALU.mult)
                        rg = rows[:, t, 0:1536].rearrange("p (g h d) -> p g h d", g=6, h=4)
                        wg = row("dswg").rearrange("p (g d) -> p g d", g=6).unsqueeze(2).broadcast_to([P, 6, 4, 64])
                        tt(rg, rg, wg, ALU.mult)
                        a, b_ = r[:, :, 0:ROT], r[:, :, ROT:2 * ROT]
                        cc = cosr[:, t, :].unsqueeze(1).broadcast_to([P, 24, ROT])
                        ss = sinr[:, t, :].unsqueeze(1).broadcast_to([P, 24, ROT])
                        w = [D_SQ[:, i * 192:(i + 1) * 192].rearrange("p (n j) -> p n j", n=24) for i in range(4)]
                        for o, i0, i1 in ((w[0], a, cc), (w[1], b_, ss), (w[2], b_, cc), (w[3], a, ss)):
                            tt(o, i0, i1, ALU.mult)
                        tt(a, w[0], w[1], ALU.subtract)
                        tt(b_, w[2], w[3], ALU.add, c=gave_pe if t else step)
                    attention(DG, ("dswP", qd), dmask[:, :, :], 0.125, qd, rows, 3 * DG * UC)
                add_rows("dsw2o")

            setup()
            mixer(0)
            if want("ffn0"):
                ffn(0)
            if want("mix1"):
                mixer(1)
            if want("moe"):
                ffn(1)
            if want("fox"):
                fox()
            if want("dsw"):
                dsw()
            v.memset(junk[:, 0:1], 0.0).then_inc(out_ready, 1)


def unit_of(w, c0, n=UC):
    k = w.shape[0] // P
    return w[:, c0:c0 + n].reshape(k, P, n).transpose(1, 0, 2).reshape(P, k * n)


def columns(a):
    return np.asarray(a).reshape(-1, P).T


def lay_out(inp):
    before, experts, after = stream_plan()
    units = before + experts + after
    stream = np.empty((len(units), P, UNIT), np.float32)
    w_in, w_branch, w_out, w_mod = inp["w_in"], inp["w_branch"], inp["w_out"], inp["w_mod"]
    starts = {n: [c for lo, hi in spans for c in range(lo, hi, UC)]
              for n, spans in (("a", W_IN_A), ("b", W_IN_B), ("c", W_IN_C))}
    ffns = {"f": [inp[n] for n in ("ffn_w1", "ffn_w3", "ffn_w2")],
            "m": [inp[n][0] for n in ("moe_w1", "moe_w3", "moe_w2")]}
    for u, (name, l, j) in enumerate(units):
        if name == "mod":
            stream[u] = unit_of(w_mod[l], j * UC)
        elif name in starts:
            stream[u] = unit_of(w_in[l], starts[name][j])
        elif name == "gate":
            stream[u] = unit_of(w_in[l], W_IN_GATE + j * UC)
        elif name == "branch":
            stream[u] = unit_of(w_branch[l, j // 2], (j % 2) * 512, 512)
        elif name == "out":
            stream[u] = unit_of(w_out[l], j * UC)
        elif name[:2] in ("w1", "w3"):
            stream[u] = unit_of(ffns[name[2]][name[1] == "3"][l], j * UC)
        elif name[:2] == "w2":
            stream[u] = unit_of(ffns[name[2]][2][l][j * UC:(j + 1) * UC], 0, D)
        elif name == "fox":
            stream[u] = unit_of(inp["fox_w_in_2"][0], (j % 4) * D + (j // 4) * UC)
        elif name == "foxo":
            stream[u] = unit_of(inp["fox_w_out_2"][0], j * UC)
        elif name == "dsw":
            stream[u] = unit_of(inp["dsw_w_in_2"][0], (j % 10) * D + (j // 10) * UC)
        elif name == "dswo":
            stream[u] = unit_of(inp["dsw_w_out_2"][0], j * UC)
    cols = np.zeros((P, N_COLS), np.float32)

    def put(name, a, lo=0):
        o = COLS[name][0] + lo
        cols[0:a.shape[0], o:o + a.shape[1]] = a

    put("c", columns(inp["c"]))
    put("ng", columns(inp["norm_g_2"].reshape(-1)))
    for l in range(DEPTH):
        put("bmod", columns(inp["b_mod"][l]), l * 48)
        put("n1", columns(inp["norm1_w"][l]), l * KC)
        put("n2", columns(inp["norm2_w"][l]), l * KC)
        put("convw", inp["c_conv_w"][l].reshape(4, 8, P).transpose(2, 1, 0).reshape(P, 32), l * 32)
        put("convb", columns(inp["c_conv_b"][l]), l * 8)
        for name, key in (("aq", "a_qnorm_w"), ("ak", "a_knorm_w")):
            put(name, np.concatenate([inp[key][l]] * 2)[:, None], l)
        for name, key in (("subln", "a_subln_w"), ("gnorm", "b_gnorm_w"), ("cnorm", "c_norm_w"),
                          ("ib", "c_igate_b"), ("fb", "c_fgate_b")):
            put(name, inp[key][l][:, None], l)
        put("lb", columns(inp["b_lb_logits"][l]), l * HEADS)
        put("wif", unit_of(w_in[l], W_IN_IF, 8), l * KC * 8)
    put("router", unit_of(inp["moe_router_w"][0], 0, NE))
    put("foxwf", unit_of(inp["fox_w_in_2"][0], 4 * D, 16))
    put("foxq", inp["fox_q_norm_2"][0][:, None])
    put("foxk", inp["fox_k_norm_2"][0][:, None])
    lam = np.stack([inp[f"a_lambda_{n}"] for n in ("q1", "k1", "q2", "k2")], axis=1).reshape(-1)
    rows = np.concatenate([lam, inp["moe_router_b"].reshape(-1), inp["fox_b_f_2"].reshape(-1),
                           inp["dsw_q_norm_2"].reshape(-1), inp["dsw_k_norm_2"].reshape(-1)])[None, :]
    bgate = np.concatenate([inp["b_mod"][:, 2 * D:3 * D], inp["b_mod"][:, 5 * D:6 * D]], axis=1)
    return {"stream": stream, "cols": cols, "rows": rows, "bgate": bgate, "x": inp["x"][0],
            "pos": inp["positions_2"].reshape(T, P).T}


def kernel(**inputs):
    import concourse.bacc as bacc
    from concourse.bass_utils import run_bass_kernel_spmd

    nc = bacc.Bacc("TRN2", target_bir_lowering=False, num_devices=1)
    arrays = {k: np.ascontiguousarray(a)
              for k, a in lay_out({k: np.asarray(v) for k, v in inputs.items()}).items()}
    args = [nc.dram_tensor(k, a.shape, mybir.dt.from_np(a.dtype), kind="ExternalInput").ap()
            for k, a in arrays.items()]
    out = nc.dram_tensor("out", (S, D), F32, kind="ExternalOutput").ap()
    two_blocks(nc, *args, out)
    r = run_bass_kernel_spmd(nc, [arrays], core_ids=[0])
    return r.results[0]["out"].reshape(1, S, D)
```

```python
import math
from contextlib import ExitStack, contextmanager

import numpy as np

import concourse.bass as bass
from concourse import mybir

F32 = mybir.dt.float32
I32 = mybir.dt.int32
ACT = mybir.ActivationFunctionType
ALU = mybir.AluOpType
X = mybir.AxisListType.X

P = 128
D = 1024
KC = D // P
T = 2
S = T * P
DEPTH = 2
UNIT = 2048
UC = UNIT // KC
RING = 11
RING_MIX = 7
D_FF = 2816
FG = D_FF // UC
NE = 8
EXPERT_UNITS = 3 * FG
EPS = 1e-6
NEG = -1e30
HEADS = 4
AK = 64
HD = 128
SLOPES = [2.0 ** (-8.0 * i / HEADS) for i in range(1, HEADS + 1)]
LEVELS = [64, 32, 16, 8, 4, 2, 1]
QUADS = 4
DG = 3
DILATIONS = (1, 4, 16)
ROT = 8
CV = HD + 1
C_UNITS = 8
FOX_UNITS = [[0], [1], [2], [], [3], [], [], []]
DSW_UNITS = [[0, 1], [2, 3], [4, 5], [6], [7], [8], [9], []]
NORM_STEP = 2
TURN_STEP = 5

W_IN_A = [(0, 1024), (1024, 1536)]
W_IN_B = [(2048, 2560), (1536, 2048), (2560, 3584)]
W_IN_C = [(3584, 4608), (4608, 5632)]
W_IN_IF = 5632
W_IN_GATE = 5640

COLS = {}
for _name, _n in [("c", KC), ("bmod", 2 * 48), ("n1", 2 * KC), ("n2", 2 * KC), ("router", KC * NE),
                  ("convw", 2 * 32), ("convb", 2 * 8), ("aq", 2), ("ak", 2), ("subln", 2), ("gnorm", 2),
                  ("cnorm", 2), ("lb", 2 * HEADS), ("wif", 2 * KC * 8), ("ng", 2 * KC), ("foxwf", KC * 16),
                  ("foxq", 1), ("foxk", 1), ("ib", 2), ("fb", 2)]:
    COLS[_name] = (sum(n for _, n in COLS.values()), _n)
N_COLS = sum(n for _, n in COLS.values())
ROWS = {}
for _name, _n in [("lam", 2 * 4 * AK), ("rb", NE), ("foxbf", 16), ("dswg", 2 * DG * 64)]:
    ROWS[_name] = (sum(n for _, n in ROWS.values()), _n)
N_ROWS = sum(n for _, n in ROWS.values())


def stream_plan():
    def mixer(l):
        parts = [("mod", 0, 8), ("a", 0, 6), ("b", 0, 8), ("mod", 8, 24), ("c", 0, 8), ("gate", 0, 8),
                 ("branch", 0, 2), ("gate", 8, 12), ("branch", 2, 6), ("out", 0, 4)]
        return [(name, l, j) for name, lo, hi in parts for j in range(lo, hi)]

    def ffn(name, e):
        u = [("w1" + name, e, 0), ("w3" + name, e, 0)]
        for g in range(1, FG):
            u += [("w1" + name, e, g), ("w3" + name, e, g), ("w2" + name, e, g - 1)]
        return u + [("w2" + name, e, FG - 1)]

    before = mixer(0) + ffn("f", 0) + mixer(1)
    experts = [u for e in range(NE) for u in ffn("m", e)]
    after = [("fox", 0, j) for j in range(4 * QUADS)] + [("foxo", 0, j) for j in range(4)]
    after += [("dsw", 0, j) for j in range((3 * DG + 1) * QUADS)] + [("dswo", 0, j) for j in range(4)]
    return before, experts, after


def ring_plan():
    before, experts, after = stream_plan()
    experts = experts * 2
    fills, last, out = [0] * RING, [None] * RING, []
    at = 0
    for name, _, _ in before + experts + after:
        n = RING if name[:2] in ("w1", "w2", "w3") else RING_MIX
        if out and n != kind:
            at = 0
        kind, s = n, at % n
        fills[s] += 1
        out.append((s, fills[s], last[s]))
        last[s] = len(out) - 1
        at += 1
    return out


class Count:

    def __init__(self, sem):
        self.sem, self.n, self.turn = sem, 0, 0

    def more(self, n=1):
        self.n += n
        return self.sem, self.n + self.turn

    def at(self, n):
        return self.sem, n + self.turn


@contextmanager
def turns(eng, times, per):
    with eng.Fori(0, times) as i:
        start = {c: c.n for c in per}
        for c, n in per.items():
            c.turn = i * n
        yield i
        for c, n in per.items():
            assert c.n - start[c] == n, (c.sem, c.n - start[c], n)
            c.turn, c.n = 0, start[c] + n * times


def two_blocks(nc, stream, cols_d, rows_d, bgate_d, x_d, pos_d, out_d, stop=None):
    n_before, n_experts, n_after = (len(u) for u in stream_plan())
    plan = ring_plan()
    ctx = ExitStack()
    with ctx:
        def sb(name, *shape, dt=F32):
            return ctx.enter_context(nc.sbuf_tensor(name, list(shape), dt))

        def sem(name):
            return ctx.enter_context(nc.semaphore(name))

        ring = sb("ring", P, RING, UNIT)
        W = ring[:, RING_MIX:RING, :].rearrange("p a b -> p (a b)")
        x = sb("x_rows", P, T, D)
        hT = sb("hT", P, KC, S)
        RW = 2560
        RA = sb("RA", P, T, RW)
        RB = sb("RB", P, T, RW)
        YT = sb("YT", P, 3, HEADS, S)
        QT2 = sb("QT2", P, 3072)
        gates_row = sb("gates_row", P, 2, D)
        colt = sb("colt", P, N_COLS)
        rowt = sb("rowt", P, N_ROWS)
        ident = sb("ident", P, P)
        ones = sb("ones", P, P)
        tri = sb("tri", P, P)
        causal = sb("causal", P, S)
        causalT = sb("causalT", P, P)
        dist = sb("dist", P, S)
        lev = sb("lev", P, len(LEVELS), P)
        dmask = sb("dmask", P, DG, S)
        sel = sb("sel", HEADS, HEADS, P)
        cond = sb("cond", P, KC)
        modc = sb("modc", P, 48)
        A1 = sb("A1", P, KC)
        A2 = sb("A2", P, KC)
        junk = sb("junk", P, P)
        small = sb("small", P, 512)
        lamt = sb("lamt", P, 8)
        lbc = sb("lbc", P, 6, HEADS)
        qc66 = sb("qc66", P, 2)
        aT_sb = sb("aT_sb", P, 2, P)
        comb = sb("comb", P, T, NE)
        cosr = sb("cosr", P, T, ROT)
        sinr = sb("sinr", P, T, ROT)
        posi = sb("posi", P, T, dt=I32)
        idx = sb("idx", P, S, dt=I32)
        idx2 = sb("idx2", P, S, dt=I32)
        iotaf = sb("iotaf", P, P)
        most = sb("most", P, 1, dt=I32)
        negS = small[:, 192:200]
        sumS = small[:, 200:208]
        recS = small[:, 208:216]
        meansq = small[:, 128:176]
        ssx = small[:, 448:450]
        ps = ctx.enter_context(nc.psum_tensor("ps", [P, 8, 512], F32))
        psS = [ps[:, 4:6, :].rearrange("p a b -> p (a b)"), ps[:, 6:8, :].rearrange("p a b -> p (a b)")]

        def col(name, lo=0, n=1):
            o = COLS[name][0] + lo
            return colt[:, o:o + n]

        def row(name):
            o, n = ROWS[name]
            return rowt[:, o:o + n]

        landed = [sem(f"landed{s}") for s in range(RING)]
        unit_done = sem("unit_done")
        burst_for_dve = sem("burst_for_dve")
        burst_for_act = sem("burst_for_act")
        dve_took = sem("dve_took")
        act_took = sem("act_took")
        dve_gave_pe = sem("dve_gave_pe")
        act_gave_pe = sem("act_gave_pe")
        dve_gave_act = sem("dve_gave_act")
        act_gave_dve = sem("act_gave_dve")
        dve_step = sem("dve_step")
        act_step = sem("act_step")
        pool_step = sem("pool_step")
        most_known = sem("most_known")
        masks_made = sem("masks_made")
        inputs_in = sem("inputs_in")
        bgate_in = sem("bgate_in")
        work_free = sem("work_free")
        gates_free = sem("gates_free")
        out_ready = sem("out_ready")
        out_written = sem("out_written")

        ticket = {}

        stages = ["mix0", "ffn0", "mix1", "moe", "fox", "dsw"]
        last = stages.index(stop) if stop else len(stages) - 1

        gain = {unit_done: EXPERT_UNITS, burst_for_act: FG + 1, burst_for_dve: 4,
                act_took: 2 * FG + 1, dve_took: FG + 5, dve_gave_pe: 2, dve_step: 12}
        full = {}

        def bank_of(eng, key, turn=None):
            bank, s, v = full[key]
            eng.wait_ge(s, v if turn is None else turn * gain[s] + v)
            return bank

        A_QT = W[:, 0:2048].rearrange("p (b s) -> p b s", b=8)
        A_SQ = W[:, 2048:3072]
        COND = W[:, 3072:4096].rearrange("p (k n) -> p k n", k=KC)
        A_S = W[:, 4096:4608]
        A_E = W[:, 4608:5120]
        A_W = W[:, 5120:5632].rearrange("p (n k) -> p n k", n=2)
        Y_A = W[:, 5632:6656].rearrange("p (t h d) -> p t h d", t=T, h=HEADS)

        def heads_T(a):
            return W[:, a:a + 1024].rearrange("p (h s) -> p h s", h=HEADS)

        B_Q, B_K, B_B, B_E, B_QP, B_KP = (heads_T(1024 * i) for i in range(6))
        B_ATT = W[:, 6144:7168].rearrange("p (t h s) -> p t h s", t=T, h=HEADS)
        B_ATTX = W[:, 7168:7680].rearrange("p (h s) -> p h s", h=HEADS)
        B_TMP = W[:, 7680:8192]
        Y_B = W[:, 0:1024].rearrange("p (t h d) -> p t h d", t=T, h=HEADS)
        C_PAD = W[:, 0:2080].rearrange("p (b s) -> p b s", b=8)
        C_M = heads_T(0)
        C_QK = W[:, 2080:4128].rearrange("p (b s) -> p b s", b=8)
        C_R4, C_EM4, C_M4 = (W[0:4, a:a + S] for a in (4608, 4864, 5120))
        C_F4, C_B4, C_I4 = (W[0:4, a:a + S] for a in (6528, 6784, 7168))
        C_G, C_E, C_W = (W[:, a:a + 384] for a in (5376, 5760, 6144))
        Y_C = W[:, 7168:8192].rearrange("p (t h d) -> p t h d", t=T, h=HEADS)
        D_S = [W[:, a:a + 768].rearrange("p (g k) -> p g k", g=DG) for a in (3104, 3872)]
        PR = [W[:, a:a + 768].rearrange("p (g k) -> p g k", g=DG) for a in (4864, 5632)]
        PT = [a.rearrange("p (k g q) -> p k g q", k=T, g=DG)
              for a in (W[:, 6400:7168], gates_row[:, 0, 0:768])]
        D_SQ = W[:, 7168:8192]
        F_QA = W[:, 0:1056].rearrange("p (t v d) -> p t v d", t=T, v=8)
        F_QT = [a.rearrange("p (v s) -> p v s", v=8) for a in (W[:, 1056:3104], QT2[:, 0:2048])]
        D_QT = [a.rearrange("p (v s) -> p v s", v=12) for a in (W[:, 0:3072], QT2[:, :])]
        OG = YT[:, :, :, :].rearrange("p b h s -> p (b h s)")[:, 0:T * D].rearrange("p (t d) -> p t d", t=T)
        gate_h = RA[:, 0, 0:1024].rearrange("p (n c) -> p n c", n=2)
        hid = RA[:, 0, 1024:2048].rearrange("p (n t c) -> p n t c", n=2, t=T)
        actT = RA[:, 1, 0:1024].rearrange("p (n k s) -> p n k s", n=2, k=2)
        moe_sum = RB[:, :, 1024:2048]
        flatY = YT[:, :, :, :].rearrange("p b h s -> p (b h s)")
        slot_rows = flatY[:, 0:D]
        pick = flatY[:, D:D + S].rearrange("p (t s) -> p t s", t=T)
        pick_w = flatY[:, D + S:D + 2 * S].rearrange("p (t s) -> p t s", t=T)
        spread = flatY[:, D + 2 * S:D + 3 * S]
        route = lambda o, n: small[:, o:o + T * n].rearrange("p (t e) -> p t e", t=T)
        pos9, w9 = route(300, NE + 1), route(320, NE + 1)
        pos_all, w_all, chosen = route(340, NE), route(356, NE), route(372, NE)

        def want(stage):
            return stages.index(stage) <= last

        ATT = [(t, h) for t in range(T) for h in range(4)]

        block = ctx.enter_context(nc.Block())

        @block.tensor
        def _(pe):
            done = Count(unit_done)
            for_dve, for_act = Count(burst_for_dve), Count(burst_for_act)
            took = {"dve": Count(dve_took), "act": Count(act_took)}
            from_dve, from_act = Count(dve_gave_pe), Count(act_gave_pe)
            freed = {}
            state = {"unit": 0, "U": 0, "T": 0, "S": 0}

            def free(bank):
                if bank in freed:
                    c, n = freed[bank]
                    pe.wait_ge(*c.at(n))

            def taken_by(who, banks, key):
                c = took[who]
                c.more()
                for b in banks:
                    freed[b] = (c, c.n)
                ticket[key] = (who, c.n)

            def need(key):
                who, n = ticket[key]
                pe.wait_ge(*took[who].at(n))

            def next_bank(kind):
                banks = {"U": [0, 1], "T": [2, 3], "S": [4, 6]}[kind]
                b = banks[state[kind] % 2]
                state[kind] += 1
                free(b)
                if kind == "S":
                    free(b + 1)
                return b

            def landed_unit(turn=None, base_fill=None):
                u = state["unit"]
                state["unit"] += 1
                s, fill, _ = plan[u]
                if turn is None:
                    pe.wait_ge(landed[s], 16 * fill)
                else:
                    pe.wait_ge(landed[s], turn * (16 * 3) + 16 * fill)
                return s

            def rows_unit(who, key, turn=None, tiles=T, lhs=None):
                lhs = hT if lhs is None else lhs
                s = landed_unit(turn)
                b = next_bank("U")
                for t in range(tiles):
                    for k in range(KC):
                        m = pe.matmul(ps[:, b, t * UC:(t + 1) * UC], lhs[:, k, t * P:(t + 1) * P],
                                      ring[:, s, k * UC:(k + 1) * UC], start=k == 0, stop=k == KC - 1)
                m.then_inc(unit_done, 1)
                unit_full(who, [b], key)

            def unit_full(who, banks, key):
                done.more()
                full[key] = (banks[0], unit_done, done.n)
                taken_by(who, banks, key)

            def finish(m, who, banks, key):
                c, sem_ = (for_dve, burst_for_dve) if who == "dve" else (for_act, burst_for_act)
                c.more()
                m.then_inc(sem_, 1)
                full[key] = (banks[0], sem_, c.n)
                taken_by(who, banks, key)

            def transposes(who, key, ins, width=P):
                b = next_bank("T")
                for i, a in enumerate(ins):
                    m = pe.transpose(ps[0:width, b, i * P:(i + 1) * P], a, ident[:, :])
                finish(m, who, [b], key)

            def norm_T(tag, src):
                for t in range(T):
                    pe.wait_ge(*from_dve.more())
                    for g in range(2):
                        transposes("dve", (tag, t, g),
                                   [src[:, t, (4 * g + i) * P:(4 * g + i + 1) * P] for i in range(4)])
                need((tag, T - 1, 1))

            def mod(l, units):
                for j in units:
                    s = landed_unit()
                    b = next_bank("U")
                    for k in range(KC):
                        m = pe.matmul(ps[:, b, 0:UC], COND[:, k, :], ring[:, s, k * UC:(k + 1) * UC],
                                      start=k == 0, stop=k == KC - 1)
                    m.then_inc(unit_done, 1)
                    unit_full("dve", [b], ("mod", l, j))

            def diff_attention(l):
                QT = A_QT
                for t in range(T):
                    pe.wait_ge(*from_dve.more())
                    for g in range(2):
                        transposes("dve", ("aT", l, t, g),
                                   [RA[:, t, (4 * g + i) * P:(4 * g + i + 1) * P] for i in range(4)])
                need(("aT", l, T - 1, 1))
                for t in range(T):
                    nk = (t + 1) * P

                    def score(h):
                        b = next_bank("S")
                        r = 64 * (h % 2)
                        for m_ in range(2):
                            m = pe.matmul(ps[:, b, m_ * nk:(m_ + 1) * nk],
                                          QT[r:r + AK, 2 * m_ + h // 2, t * P:(t + 1) * P],
                                          QT[r:r + AK, 4 + 2 * m_ + h // 2, 0:nk], start=True, stop=True)
                        finish(m, "dve", [b], ("aS", l, t, h))

                    score(0)
                    bo = 5 + 2 * t
                    for h in range(HEADS):
                        if h + 1 < HEADS:
                            score(h + 1)
                        n = 8 + 2 * (HEADS * t + h)
                        mod(l, range(n, n + 2))
                        pe.wait_ge(*from_dve.more())
                        a = A_W[:, h % 2, :]
                        transposes("act", ("aA", l, t, h), [a[:, i * P:(i + 1) * P] for i in range(t + 1)])
                        need(("aA", l, t, h))
                        if h == 0:
                            free(bo)
                        for kt in range(t + 1):
                            m = pe.matmul(ps[:, bo, h * HD:(h + 1) * HD], aT_sb[:, kt, :],
                                          RA[:, kt, 1024 + h * HD:1024 + (h + 1) * HD],
                                          start=kt == 0, stop=kt == t)
                    finish(m, "dve", [bo], ("aO", l, t))

            def y_T(l, br):
                for t in range(T):
                    pe.wait_ge(*from_dve.more())
                    transposes("dve", ("yT", l, br, t), [(Y_A, Y_B, Y_C)[br][:, t, i, :] for i in range(4)])

            def hgrn(l):
                Qb, Kb, Qp, Kp, att, attx = B_Q, B_K, B_QP, B_KP, B_ATT, B_ATTX
                for i in range(2):
                    for t in range(T):
                        transposes("act", ("bT", l, i, t),
                                   [RB[:, t, 512 * i + j * P:512 * i + (j + 1) * P] for j in range(4)])
                y_T(l, 0)
                rows_unit("act", ("c", l, 0))
                for n in range(len(LEVELS) + 1):
                    if n + 1 < C_UNITS:
                        rows_unit("act", ("c", l, n + 1))
                    else:
                        gates(l, range(0, 1))
                    pe.wait_ge(*from_dve.more())
                    q, k = (Qb, Kb) if n == 0 else (Qp, Kp)
                    for t in range(T):
                        b = next_bank("S")
                        for h in range(HEADS):
                            m = pe.matmul(ps[:, b, h * P:(h + 1) * P], k[:, h, t * P:(t + 1) * P],
                                          q[:, h, t * P:(t + 1) * P], start=True, stop=True)
                        finish(m, "dve", [b, b + 1], ("lev", l, n, t))
                gates(l, range(1, 2))
                pe.wait_ge(*from_dve.more())
                b = next_bank("S")
                for h in range(HEADS):
                    m = pe.matmul(ps[:, b, h * P:(h + 1) * P], Kp[:, h, 0:P], Qp[:, h, P:S],
                                  start=True, stop=True)
                finish(m, "dve", [b, b + 1], ("levx", l))
                need(("levx", l))
                for t in range(T):
                    b = next_bank("S")
                    for h in range(HEADS):
                        o = ps[:, b, h * HD:(h + 1) * HD]
                        vv = lambda t_: RB[:, t_, 1024 + h * HD:1024 + (h + 1) * HD]
                        m = pe.matmul(o, att[:, t, h, :], vv(t), start=True, stop=t == 0)
                        if t == 1:
                            m = pe.matmul(o, attx[:, h, :], vv(0), start=False, stop=True)
                    finish(m, "dve", [b, b + 1], ("bO", l, t))

            def gates(l, units):
                for j in units:
                    rows_unit("act", ("gate", l, j))

            def gate_logits(l):
                b = next_bank("T")
                for i in range(2):
                    for k in range(KC):
                        w = col("wif", (l * KC + k) * 8 + 4 * i, 4)
                        m = pe.matmul(ps[0:4, b, i * S:(i + 1) * S], w, hT[:, k, :],
                                      start=k == 0, stop=k == KC - 1)
                finish(m, "dve", [b], ("cG", l))

            def mlstm(l):
                gate_logits(l)
                QK, r4, em4, M4 = C_QK, C_R4, C_EM4, C_M4
                for t in range(T):
                    for g in range(2):
                        transposes("act", ("cT", l, t, g),
                                   [RA[:, t, (4 * g + i) * P:(4 * g + i + 1) * P] for i in range(4)])
                gates(l, range(3, 6))
                pe.wait_ge(*from_act.more())
                b = next_bank("T")
                for i, a in enumerate((r4, em4)):
                    for t in range(T):
                        m = pe.transpose(ps[:, b, (2 * i + t) * 4:(2 * i + t) * 4 + 4],
                                         a[:, t * P:(t + 1) * P], ident[0:4, 0:4])
                finish(m, "dve", [b], ("cR", l))
                for hp in range(2):
                    b = next_bank("T")
                    for i in range(2):
                        m = pe.matmul(ps[:, b, i * S:(i + 1) * S], sel[:, 2 * hp + i, :], M4,
                                      start=True, stop=True)
                    finish(m, "dve", [b], ("cM", l, hp))
                pe.wait_ge(*from_act.more())
                for h in range(HEADS):
                    b = next_bank("S")
                    pe.matmul(ps[:, b, 0:S], QK[:, 4 + h, 0:P], QK[:, h, :], start=True, stop=True)
                    m = pe.matmul(ps[:, b, S:S + P], QK[:, 4 + h, P:S], QK[:, h, P:S], start=True, stop=True)
                    finish(m, "dve", [b, b + 1], ("cw", l, h))
                    gates(l, range(min(6 + h, C_UNITS), min(7 + h, C_UNITS)))
                    need(("cw", l, h))
                    Wt = C_W
                    vv = lambda t_: RA[:, t_, 1024 + h * CV:1024 + (h + 1) * CV]
                    b = next_bank("T")
                    pe.matmul(ps[:, b, 0:CV], Wt[:, 0:P], vv(0), start=True, stop=True)
                    pe.matmul(ps[:, b, 256:256 + CV], Wt[:, P:2 * P], vv(0), start=True, stop=False)
                    m = pe.matmul(ps[:, b, 256:256 + CV], Wt[:, 2 * P:3 * P], vv(1), start=False, stop=True)
                    finish(m, "dve", [b], ("cO", l, h))

            def merge(l, br):
                need(("yT", l, br, T - 1))
                for j in range(2):
                    s = landed_unit()
                    b = next_bank("S")
                    for t in range(T):
                        for k in range(4):
                            m = pe.matmul(ps[:, b + t, :], YT[:, br, k, t * P:(t + 1) * P],
                                          ring[:, s, k * 512:(k + 1) * 512], start=k == 0, stop=k == 3)
                    m.then_inc(unit_done, 1)
                    unit_full("dve", [b, b + 1], ("branch", l, br, j))

            def project(tag, src_ready):
                for t in range(T):
                    pe.wait_ge(*from_dve.more())
                    for g in range(2):
                        transposes("act", (tag, t, g), [src_ready(t, 4 * g + i) for i in range(4)])
                need((tag, T - 1, 1))
                for j in range(4):
                    rows_unit("dve", (tag + "o", j))

            def mixer(l):
                pe.wait_ge(*from_dve.more())
                mod(l, range(8))
                if l == 0:
                    pe.wait_ge(masks_made, 1)
                norm_T(f"n1{l}", RB)
                for j in range(6):
                    rows_unit("act", ("a", l, j))
                for j in range(8):
                    rows_unit("act", ("b", l, j))
                diff_attention(l)
                hgrn(l)
                gates(l, range(2, 3))
                y_T(l, 1)
                mlstm(l)
                merge(l, 0)
                gates(l, range(8, 12))
                y_T(l, 2)
                merge(l, 1)
                merge(l, 2)
                project(f"m{l}", lambda t, i: RA[:, t, i * P:(i + 1) * P])

            def gather(l, first):
                pe.wait_ge(*from_dve.more())
                for g in range(2):
                    b = next_bank("T")
                    for i in range(4):
                        for t in range(T):
                            k = 4 * g + i
                            m = pe.matmul(ps[:, b, i * P:(i + 1) * P], RB[:, t, k * P:(k + 1) * P], pick[:, t, :],
                                          start=t == 0, stop=t == T - 1)
                    finish(m, "dve", [b], ("pick0" if first else "pick", l, g))

            def scatter(l):
                need(("y", l, 0))
                need(("spread", l))
                for t in range(T):
                    b = 6 - 2 * t
                    free(b)
                    for n in range(2):
                        m = pe.matmul(ps[:, b + n, :], spread[:, t * P:(t + 1) * P],
                                      slot_rows[:, n * 512:(n + 1) * 512], start=True, stop=True)
                    finish(m, "dve", [b, b + 1], ("back", l, t))

            def swiglu(l, turn=None):
                tiles = T if turn is None else 1

                def down(g):
                    s = landed_unit(turn)
                    need(("act", l, g))
                    for t in range(tiles):
                        for n in range(2):
                            if g == 0:
                                free(4 + 2 * t + n)
                            for k in range(2):
                                m = pe.matmul(ps[:, 4 + 2 * t + n, :], actT[:, g % 2, k, t * P:(t + 1) * P],
                                              ring[:, s, k * D + n * 512:k * D + n * 512 + 512],
                                              start=g == 0 and k == 0, stop=g == FG - 1 and k == 1)
                    m.then_inc(unit_done, 1)
                    done.more()
                    full["y", l] = (4, unit_done, done.n)

                def turn_rows(g):
                    need(("w3", l, g))
                    transposes("act", ("act", l, g), [hid[:, g % 2, t, k * P:(k + 1) * P]
                                                   for k in range(2) for t in range(tiles)])

                for g in range(FG):
                    rows_unit("act", ("w1", l, g), turn, tiles)
                    if g >= 1:
                        turn_rows(g - 1)
                    rows_unit("dve", ("w3", l, g), turn, tiles)
                    if turn is not None and g == 2:
                        pe.wait_ge(*from_dve.more())
                        transposes("act", ("spread", l), [pick_w[:, t, :] for t in range(T)])
                    if turn is not None and g == FG - 1:
                        gather(l, False)
                    if g >= 1:
                        down(g - 1)
                turn_rows(FG - 1)
                down(FG - 1)
                for t in range(tiles):
                    taken_by("dve", [4 + 2 * t, 5 + 2 * t], ("y", l, t))
                if turn is not None:
                    scatter(l)

            def ffn(l):
                norm_T(f"n2{l}", RB)
                if l == 0:
                    swiglu(l)
                    return
                b = next_bank("T")
                for t in range(T):
                    for k in range(KC):
                        m = pe.matmul(ps[:, b, t * NE:(t + 1) * NE], hT[:, k, t * P:(t + 1) * P],
                                      col("router", k * NE, NE), start=k == 0, stop=k == KC - 1)
                finish(m, "dve", [b], "router")
                pe.wait_ge(*from_dve.more())
                b = next_bank("T")
                o = ps[:, b, 0:T * NE].rearrange("p (t e) -> p t e", t=T)
                pe.matmul(o[:, 0, :], tri[:, :], chosen[:, 0, :], start=True, stop=True)
                pe.matmul(o[:, 1, :], ones[:, :], chosen[:, 0, :], start=True, stop=False)
                pe.matmul(o[:, 1, :], tri[:, :], chosen[:, 1, :], start=False, stop=True)
                for t in range(T):
                    m = pe.matmul(ps[:, b, T * NE:(T + 1) * NE], ones[:, :], chosen[:, t, :],
                                  start=t == 0, stop=t == T - 1)
                finish(m, "dve", [b], "count")
                experts(1)
                pe.wait_ge(unit_done, done.n)
                pe.wait_ge(most_known, 1)
                more = pe.value_load(most[0:1, 0:1], min_val=0, max_val=S)
                before = {c: c.n for c in (done, for_act, for_dve)}
                with pe.If(more > P):
                    experts(2)
                with pe.Else():
                    for c, n in before.items():
                        pe.sem_inc(c.sem, c.n - n)

            def all_taken():
                for c in took.values():
                    pe.wait_ge(c.sem, c.n)
                freed.clear()

            def experts(l):
                all_taken()
                state["T"] = 0
                gather(l, True)
                all_taken()
                state["U"] = state["T"] = 0
                d0, a0 = took["dve"].n, took["act"].n
                with turns(pe, NE, {c: gain[c.sem] for c in
                                    (done, for_act, for_dve, took["dve"], took["act"], from_dve)}) as i:
                    u0 = state["unit"]
                    freed.update({0: (took["act"], a0), 1: (took["dve"], d0 - 5), 2: (took["act"], a0),
                                  3: (took["act"], a0), 4: (took["dve"], d0), 5: (took["dve"], d0),
                                  6: (took["dve"], d0 - 1), 7: (took["dve"], d0 - 1)})
                    swiglu(l, i)
                    state["unit"] = u0 + NE * EXPERT_UNITS
                all_taken()

            def attention(groups, tag, qk, val, qd, name, units, turn_rows):
                def score(n):
                    t, h = ATT[n]
                    b = next_bank("S")
                    for g in range(groups):
                        q, k = qk(h, g)
                        m = pe.matmul(psS[(b - 4) // 2][:, g * S:g * S + (t + 1) * P],
                                      q[:, t * P:(t + 1) * P], k[:, 0:(t + 1) * P], start=True, stop=True)
                    finish(m, "dve", [b, b + 1], (tag, "S", n))

                def product(n):
                    t, h = ATT[n]
                    b = next_bank("T")
                    for kt in range(t + 1):
                        need((tag, n, kt))
                        for g in range(groups):
                            m = pe.matmul(ps[:, b, 0:64], PT[n % 2][:, kt, g, :], val(kt, g, h),
                                          start=kt == 0 and g == 0, stop=kt == t and g == groups - 1)
                    finish(m, "dve", [b], (tag, "O", n))

                score(0)
                for n, (t, h) in enumerate(ATT):
                    if n + 1 < len(ATT):
                        score(n + 1)
                    if qd + 1 < QUADS:
                        for j in units[n]:
                            rows_unit("act", (name, qd + 1, j))
                    pe.wait_ge(*from_act.more())
                    pr = PR[n % 2]
                    for kt in range(t + 1):
                        transposes("act", (tag, n, kt), [pr[:, g, kt * P:(kt + 1) * P] for g in range(groups)])
                    if n:
                        product(n - 1)
                    if n == TURN_STEP and qd + 1 < QUADS:
                        turn_rows(qd + 1)
                product(len(ATT) - 1)

            def fox():
                norm_T("nfox", RB)
                b = next_bank("T")
                for t in range(T):
                    for k in range(KC):
                        m = pe.matmul(ps[:, b, t * 16:(t + 1) * 16], hT[:, k, t * P:(t + 1) * P],
                                      col("foxwf", k * 16, 16), start=k == 0, stop=k == KC - 1)
                finish(m, "dve", [b], "foxF")
                for j in range(4):
                    rows_unit("act", ("fox", 0, j))
                pe.wait_ge(*from_dve.more())
                lf = small[:, 64:96].rearrange("p (t h) -> p t h", t=T)
                b = next_bank("T")
                pe.matmul(ps[:, b, 0:16], tri[:, :], lf[:, 0, :], start=True, stop=True)
                pe.matmul(ps[:, b, 16:32], ones[:, :], lf[:, 0, :], start=True, stop=False)
                m = pe.matmul(ps[:, b, 16:32], tri[:, :], lf[:, 1, :], start=False, stop=True)
                finish(m, "dve", [b], "foxC")

                def turn_rows(qd):
                    QA = F_QA
                    pe.wait_ge(*from_dve.more())
                    for t in range(T):
                        for g in range(2):
                            transposes("dve", ("foxT", qd, t, g), [QA[:, t, 4 * g + i, :] for i in range(4)],
                                       width=66)

                turn_rows(0)
                for qd in range(QUADS):
                    rows, QT = (RA, RB)[qd % 2], F_QT[qd % 2]
                    need(("foxT", qd, T - 1, 1))
                    attention(1, ("foxP", qd), lambda h, g: (QT[0:66, h, :], QT[0:66, 4 + h, :]),
                              lambda kt, g, h: rows[:, kt, 512 + h * 64:512 + (h + 1) * 64],
                              qd, "fox", FOX_UNITS, turn_rows)
                project("fox2", lambda t, i: OG[:, t, i * P:(i + 1) * P])

            def dsw():
                norm_T("ndsw", RB)
                for j in range(3 * DG + 1):
                    rows_unit("act", ("dsw", 0, j))

                def turn_rows(qd):
                    rows = (RA, RB)[qd % 2]
                    pe.wait_ge(*from_dve.more())
                    for t in range(T):
                        for g in range(3):
                            transposes("act", ("dswT", qd, t, g),
                                       [rows[:, t, (4 * g + i) * P:(4 * g + i + 1) * P] for i in range(4)])

                turn_rows(0)
                for qd in range(QUADS):
                    rows, QT = (RA, RB)[qd % 2], D_QT[qd % 2]
                    need(("dswT", qd, T - 1, 2))

                    def qk(h, g):
                        r = 64 * (h % 2)
                        return QT[r:r + 64, 2 * g + h // 2, :], QT[r:r + 64, 6 + 2 * g + h // 2, :]

                    attention(DG, ("dswP", qd), qk,
                              lambda kt, g, h: rows[:, kt, (6 + g) * UC + h * 64:(6 + g) * UC + (h + 1) * 64],
                              qd, "dsw", DSW_UNITS, turn_rows)
                project("dsw2", lambda t, i: OG[:, t, i * P:(i + 1) * P])

            mixer(0)
            if want("ffn0"):
                ffn(0)
            if want("mix1"):
                mixer(1)
            if want("moe"):
                ffn(1)
            if want("fox"):
                fox()
            if want("dsw"):
                dsw()
            state["end"] = state["unit"]
            ticket["units"] = state["unit"]

        @block.sync
        def _(sp):
            sp.dma_start(colt[:, :], cols_d).then_inc(inputs_in, 16)
            sp.dma_start(rowt[:, :], rows_d.broadcast_to([P, N_ROWS])).then_inc(inputs_in, 16)
            sp.dma_start(gates_row[:, :, :].rearrange("p a b -> p (a b)"),
                         bgate_d[0:1, :].broadcast_to([P, 2 * D])).then_inc(bgate_in, 16)
            sp.dma_start(posi[:, :], pos_d).then_inc(inputs_in, 16)
            for t in range(T):
                sp.dma_start(x[:, t, :], x_d[t * P:(t + 1) * P, :]).then_inc(inputs_in, 16)
            units = ticket["units"]

            def kind(u):
                return 0 if u is None else 2 if u >= n_before else 1

            def load(u, at=None):
                s, _, prev = plan[u]
                if prev is not None:
                    sp.wait_ge(unit_done, prev + 1)
                if s >= RING_MIX and kind(u) != kind(prev):
                    sp.wait_ge(work_free, kind(u))
                sp.dma_start(ring[:, s, :], stream[u if at is None else at, :, :]).then_inc(landed[s], 16)

            u = 0
            while u < min(units, n_before):
                load(u)
                u += 1

            def expert_loads(base):
                for k in range(RING):
                    load(base + k, n_before + k)
                with sp.Fori(0, NE - 1) as i:
                    for k in range(EXPERT_UNITS):
                        s = plan[base + RING + k][0]
                        sp.wait_ge(unit_done, i * EXPERT_UNITS + (base + k + 1))
                        sp.dma_start(ring[:, s, :],
                                     stream[bass.ds(i * EXPERT_UNITS + (n_before + RING + k), 1), :, :]
                                     .squeeze(0)).then_inc(landed[s], 16)
                for k in range((NE - 1) * EXPERT_UNITS + RING, n_experts):
                    load(base + k, n_before + k)

            if units > n_before:
                expert_loads(n_before)
                for s in range(RING):
                    sp.wait_ge(landed[s], 16 * max(f for s_, f, _ in plan[:n_before + n_experts] if s_ == s))
                sp.wait_ge(most_known, 1)
                more = sp.value_load(most[0:1, 0:1], min_val=0, max_val=S)
                with sp.If(more > P):
                    expert_loads(n_before + n_experts)
                with sp.Else():
                    for s in range(RING):
                        sp.sem_inc(landed[s], 16 * (n_experts // RING))
                for u in range(n_before + 2 * n_experts, units):
                    load(u, u - n_experts)
            for t in range(T):
                sp.wait_ge(out_ready, 1)
                sp.dma_start(out_d[t * P:(t + 1) * P, :], x[:, t, :]).then_inc(out_written, 16)
            sp.wait_ge(out_written, 16 * T)

        @block.gpsimd
        def _(pool):
            n = [0]

            def link(ins):
                n[0] += 1
                ins.then_inc(pool_step, 1)
                pool.wait_ge(pool_step, n[0])

            link(pool.memset(ones[:, :], 1.0))
            link(pool.memset(ident[:, :], 0.0))
            link(pool.affine_select(out=ident[:, :], in_=ident[:, :], compare_op=ALU.not_equal, fill=1.0,
                                    base=0, pattern=[[-1, P]], channel_multiplier=1))
            link(pool.affine_select(out=tri[:, :], in_=ones[:, :], compare_op=ALU.is_ge, fill=0.0,
                                    base=0, pattern=[[1, P]], channel_multiplier=-1))
            link(pool.memset(causal[:, :], 0.0))
            link(pool.affine_select(out=causal[:, P:S], in_=causal[:, P:S], compare_op=ALU.is_ge, fill=NEG,
                                    base=0, pattern=[[-1, P]], channel_multiplier=1))
            link(pool.memset(causalT[:, :], 0.0))
            link(pool.affine_select(out=causalT[:, :], in_=causalT[:, :], compare_op=ALU.is_ge, fill=NEG,
                                    base=0, pattern=[[1, P]], channel_multiplier=-1))
            link(pool.memset(sel[:, :, :], 0.0))
            link(pool.affine_select(out=sel[:, :, :], in_=sel[:, :, :], compare_op=ALU.not_equal, fill=1.0,
                                    base=0, pattern=[[-1, HEADS], [0, P]], channel_multiplier=1))
            link(pool.iota(idx[:, :], pattern=[[-1, S]], base=P, channel_multiplier=1))
            link(pool.tensor_copy(dist[:, :], idx[:, :]))
            link(pool.tensor_scalar(dmask[:, 0, 0:P], dist[:, P:S], -1.0, None, ALU.mult))
            link(pool.affine_select(out=dist[:, P:S], in_=dist[:, P:S], compare_op=ALU.is_ge, fill=0.0,
                                    base=0, pattern=[[-1, P]], channel_multiplier=1))
            link(pool.affine_select(out=dmask[:, 0, 0:P], in_=dmask[:, 0, 0:P], compare_op=ALU.is_ge, fill=0.0,
                                    base=0, pattern=[[1, P]], channel_multiplier=-1))
            link(pool.tensor_tensor(dist[:, P:S], dist[:, P:S], dmask[:, 0, 0:P], ALU.add))
            link(pool.affine_select(out=dist[:, P + 64:S], in_=dist[:, P + 64:S], compare_op=ALU.is_ge,
                                    fill=-NEG, base=-64, pattern=[[0, 64]], channel_multiplier=1))
            link(pool.iota(idx2[:, 0:P], pattern=[[1, P]], base=0, channel_multiplier=0))
            link(pool.tensor_copy(iotaf[:, :], idx2[:, 0:P]))
            link(pool.memset(lev[:, :, :], 0.0))
            for i, m in enumerate(LEVELS):
                v = lev[:, i, :].rearrange("p (n h m) -> p n h m", h=2, m=m)[:, :, 1, :]
                link(pool.memset(v, 1.0))
                link(pool.affine_select(out=v, in_=v, compare_op=ALU.is_ge, fill=0.0, base=0,
                                        pattern=[[-2 * m, P // (2 * m)], [0, m]], channel_multiplier=1))
                link(pool.affine_select(out=v, in_=v, compare_op=ALU.is_ge, fill=0.0, base=m - 1,
                                        pattern=[[2 * m, P // (2 * m)], [0, m]], channel_multiplier=-1))
            pool.memset(junk[:, :], 0.0).then_inc(masks_made, 1)


        @block.scalar
        def _(act):
            step, took = Count(act_step), Count(act_took)
            gave_pe, gave_dve = Count(act_gave_pe), Count(act_gave_dve)
            from_dve = Count(dve_gave_act)

            def link(ins, c=step):
                ins.then_inc(c.sem, 1)
                act.wait_ge(*c.more())

            def fn(out, in_, func, **kw):
                return nc.scalar.activation(out, in_, func, **kw)

            def taken(key):
                who, n = ticket[key]
                act.wait_ge({"dve": dve_took, "act": act_took}[who], n)

            def rows_out(key, dst, func=ACT.Copy, turn=None):
                b = bank_of(act, key, turn)
                tiles = dst.shape[1]
                link(fn(dst, ps[:, b, 0:tiles * UC].rearrange("p (t c) -> p t c", t=tiles), func), took)

            def blocks_out(key, dst, n=4, turn=None):
                b = bank_of(act, key, turn)
                link(fn(dst, ps[:, b, 0:n * P].rearrange("p (n s) -> p n s", n=n), ACT.Copy), took)

            def root(a):
                act.wait_ge(*from_dve.more())
                link(fn(a, a, ACT.Sqrt), gave_dve)

            def norm_T(first=False):
                if not first:
                    act.wait_ge(*from_dve.more())
                for t in range(T):
                    link(fn(RB[:, t, 0:D], x[:, t, :], ACT.Square, accum_out=ssx[:, t:t + 1]), gave_dve)
                root(ssx)

            def softplus_of_minus_abs(dst, src, c):
                link(fn(dst, src, ACT.Abs))
                link(fn(dst, dst, ACT.Exp, scale=-1.0))
                link(fn(dst, dst, ACT.Ln, bias=1.0), c)

            def setup():
                act.wait_ge(inputs_in, 16 * 5)
                link(fn(cond[:, :], col("c", 0, KC), ACT.Silu), gave_dve)

            def constants():
                act.wait_ge(*from_dve.more())
                link(fn(lamt[:, 0:4], small[:, 0:4], ACT.Exp), gave_dve)
                act.wait_ge(*from_dve.more())
                link(fn(lbc[:, 2, :], lbc[:, 3, :], ACT.Sigmoid, scale=-1.0))
                softplus_of_minus_abs(lbc[:, 4, :], lbc[:, 3, :], gave_dve)
                act.wait_ge(*from_dve.more())
                link(fn(sinr[:, :, :], sinr[:, :, :], ACT.Sin))
                link(fn(cosr[:, :, :], cosr[:, :, :], ACT.Sin), gave_dve)

            def diff_attention(l):
                root(meansq[:, 0:32])
                for t in range(T):
                    nk = (t + 1) * P
                    for h in range(HEADS):
                        act.wait_ge(*from_dve.more())
                        link(fn(A_E[:, 0:nk], A_S[:, 0:nk], ACT.Exp, bias=negS[:, 0:1],
                                accum_out=sumS[:, 0:1]))
                        link(fn(A_E[:, nk:2 * nk], A_S[:, nk:2 * nk], ACT.Exp, bias=negS[:, 1:2],
                                accum_out=sumS[:, 1:2]), gave_dve)
                        blocks_out(("aA", l, t, h), aT_sb[:, 0:t + 1, :], t + 1)
                root(meansq[:, 0:8])

            def c_rows(l, j):
                if j < 4:
                    rows_out(("c", l, j), RA[:, :, j * UC:(j + 1) * UC])
                elif j < 6:
                    b = bank_of(act, ("c", l, j))
                    for t in range(T):
                        o = 1024 + 2 * (j - 4) * CV
                        ins = fn(RA[:, t, o:o + 2 * CV].rearrange("p (h c) -> p h c", h=2)[:, :, 0:HD],
                                 ps[:, b, t * UC:(t + 1) * UC].rearrange("p (h c) -> p h c", h=2), ACT.Copy)
                        link(ins, took if t else step)
                else:
                    rows_out(("c", l, j), RA[:, :, 1540 + (j - 6) * UC:1540 + (j - 5) * UC])

            def gates(l, units):
                for j in units:
                    rows_out(("gate", l, j), RB[:, :, j % 8 * UC:(j % 8 + 1) * UC])

            def hgrn(l):
                for i, dst in enumerate((B_B, B_Q)):
                    for t in range(T):
                        blocks_out(("bT", l, i, t), dst[:, :, t * P:(t + 1) * P])
                link(fn(B_K, B_B, ACT.Sigmoid, scale=-1.0))
                softplus_of_minus_abs(B_E, B_B, gave_dve)
                if l > 0:
                    act.wait_ge(*from_dve.more())
                    softplus_of_minus_abs(B_QP, B_QP, gave_dve)
                c_rows(l, 0)
                c_rows(l, 1)
                for i in range(len(LEVELS)):
                    act.wait_ge(*from_dve.more())
                    link(fn(B_E, B_E, ACT.Abs))
                    link(fn(B_E, B_E, ACT.Exp, scale=-1.0), gave_dve)
                    if i + 2 < C_UNITS:
                        c_rows(l, i + 2)
                    else:
                        gates(l, range(0, 1))
                act.wait_ge(*from_dve.more())
                for h in range(HEADS):
                    link(fn(B_E[:, h, 0:P], B_B[:, h, 0:P], ACT.Exp, scale=-1.0, bias=B_B[:, h, P - 1:P]))
                link(fn(B_E[:, :, P:S], B_B[:, :, P:S], ACT.Exp), gave_dve)
                gates(l, range(1, 2))
                root(meansq[:, 0:8])
                og = RA[:, :, 1540:2052]
                link(fn(og, og, ACT.Sigmoid))
                gates(l, range(2, 3))

            def mlstm(l):
                for t in range(T):
                    for g in range(2):
                        blocks_out(("cT", l, t, g), C_PAD[:, 4 * g:4 * g + 4, 3 + t * P:3 + (t + 1) * P])
                taken(("cG", l))
                softplus_of_minus_abs(C_B4, C_F4, gave_dve)
                gates(l, range(3, 6))
                act.wait_ge(*from_dve.more())
                link(fn(C_EM4, C_EM4, ACT.Exp, scale=-1.0), gave_pe)
                act.wait_ge(*from_dve.more())
                link(fn(C_QK, C_QK, ACT.Silu), gave_pe)
                for h in range(HEADS):
                    act.wait_ge(*from_dve.more())
                    link(fn(C_E[:, 0:S], C_G[:, 0:S], ACT.Exp, bias=small[:, 256 + h:257 + h]))
                    link(fn(C_E[:, S:S + P], C_G[:, S:S + P], ACT.Exp, bias=small[:, 260 + h:261 + h]), gave_dve)
                    gates(l, range(min(6 + h, C_UNITS), min(7 + h, C_UNITS)))
                root(meansq[:, 0:8])
                link(fn(RB[:, :, 0:2 * D], RB[:, :, 0:2 * D], ACT.Sigmoid), gave_dve)
                taken(("branch", l, 0, 1))
                gates(l, range(8, 12))
                link(fn(RB[:, :, 0:D], RB[:, :, 0:D], ACT.Sigmoid), gave_dve)

            def project(tag):
                for t in range(T):
                    for g in range(2):
                        blocks_out((tag, t, g), hT[:, 4 * g:4 * g + 4, t * P:(t + 1) * P])

            def mixer(l):
                norm_T(first=l == 0)
                for j in range(6):
                    if l == 0 and j == 2:
                        constants()
                    rows_out(("a", l, j), RA[:, :, j * UC:(j + 1) * UC])
                for j in range(8):
                    rows_out(("b", l, j), RB[:, :, j * UC:(j + 1) * UC],
                             ACT.Silu if j in (2, 3, 6, 7) else ACT.Copy)
                diff_attention(l)
                hgrn(l)
                mlstm(l)
                project(f"m{l}")

            def swiglu(l, turn=None):
                tiles = T if turn is None else 1

                def turned(g):
                    blocks_out(("act", l, g), actT[:, g % 2, :, 0:tiles * P].rearrange("p k (t s) -> p (k t) s", s=P),
                               2 * tiles, turn)

                for g in range(FG):
                    rows_out(("w1", l, g), gate_h[:, g % 2, 0:tiles * UC].rearrange("p (t c) -> p t c", t=tiles),
                             ACT.Silu, turn)
                    if g >= 1:
                        turned(g - 1)
                    if turn is not None and g == 2:
                        blocks_out(("spread", l), spread.rearrange("p (t s) -> p t s", t=T), T, turn)
                turned(FG - 1)

            def ffn(l):
                norm_T()
                if l == 0:
                    swiglu(l)
                    return
                act.wait_ge(*from_dve.more())
                link(fn(comb[:, :, :], comb[:, :, :], ACT.Exp), gave_dve)

                def experts(l):
                    with turns(act, NE, {took: gain[act_took]}) as i:
                        swiglu(l, i)

                experts(1)
                act.wait_ge(most_known, 1)
                more = act.value_load(most[0:1, 0:1], min_val=0, max_val=S)
                before = took.n
                with act.If(more > P):
                    experts(2)
                with act.Else():
                    act.sem_inc(act_took, took.n - before)

            def quad_unit(name, qd, j):
                rows_out((name, qd, j), (RA, RB)[qd % 2][:, :, j * UC:(j + 1) * UC])

            def gate_rows(qd, j):
                g = (RA, RB)[qd % 2][:, :, j * UC:(j + 1) * UC]
                link(fn(g, g, ACT.Silu), gave_dve)

            def attention(groups, tag, qd, name, units, turned):
                def exps(n):
                    t, _ = ATT[n]
                    act.wait_ge(*from_dve.more())
                    link(fn(PR[n % 2][:, 0:groups, 0:(t + 1) * P], D_S[n % 2][:, 0:groups, 0:(t + 1) * P],
                            ACT.Exp, bias=negS[:, n:n + 1], accum_out=sumS[:, n:n + 1]), gave_pe)

                more = qd + 1 < QUADS
                exps(0)
                for n, (t, _) in enumerate(ATT):
                    if n + 1 < len(ATT):
                        exps(n + 1)
                    for j in units[n] if more else ():
                        quad_unit(name, qd + 1, j)
                    for kt in range(t + 1):
                        blocks_out((tag, n, kt), PT[n % 2][:, kt, 0:groups, :], groups)
                    if more and n == NORM_STEP:
                        root(meansq[:, 0:16 * groups])
                    if more and n == TURN_STEP:
                        turned(qd + 1)
                if more:
                    gate_rows(qd + 1, 3 * groups)

            def fox():
                norm_T()
                taken("foxF")
                softplus_of_minus_abs(small[:, 64:96], small[:, 32:64], gave_dve)
                for j in range(4):
                    quad_unit("fox", 0, j)
                    if j == 1:
                        root(meansq[:, 0:16])
                gate_rows(0, 3)
                for qd in range(QUADS):
                    attention(1, ("foxP", qd), qd, "fox", FOX_UNITS, lambda qd: None)
                project("fox2")

            def dsw():
                norm_T()

                def turned(qd):
                    for t in range(T):
                        for g in range(3):
                            blocks_out(("dswT", qd, t, g), D_QT[qd % 2][:, 4 * g:4 * g + 4, t * P:(t + 1) * P])

                for j in range(3 * DG + 1):
                    quad_unit("dsw", 0, j)
                    if j == 6:
                        root(meansq[:, 0:48])
                gate_rows(0, 3 * DG)
                turned(0)
                for qd in range(QUADS):
                    attention(DG, ("dswP", qd), qd, "dsw", DSW_UNITS, turned)
                project("dsw2")

            setup()
            mixer(0)
            if want("ffn0"):
                ffn(0)
            if want("mix1"):
                act.wait_ge(gates_free, 1)
                act.dma_start(gates_row[:, :, :].rearrange("p a b -> p (a b)"),
                              bgate_d[1:2, :].broadcast_to([P, 2 * D])).then_inc(bgate_in, 16)
                mixer(1)
            if want("moe"):
                ffn(1)
            if want("fox"):
                fox()
            if want("dsw"):
                dsw()

        @block.vector
        def _(dve):
            step, took = Count(dve_step), Count(dve_took)
            gave_pe, gave_act = Count(dve_gave_pe), Count(dve_gave_act)
            from_act = Count(act_gave_dve)
            v = nc.vector

            def link(ins, c=step):
                ins.then_inc(c.sem, 1)
                dve.wait_ge(*c.more())

            def taken(key, turn=None):
                _, n = ticket[key]
                dve.wait_ge(act_took, n if turn is None else turn * gain[act_took] + n)

            def tt(out, a, b, op, c=step):
                link(v.tensor_tensor(out, a, b, op), c)

            def ts(out, a, s1, s2, op0, op1=None, c=step):
                if op1 is None:
                    link(v.tensor_scalar(out, a, s1, None, op0), c)
                else:
                    link(v.tensor_scalar(out, a, s1, s2, op0, op1), c)

            def stt(out, a, s_, b, op0, op1, c=step):
                link(v.scalar_tensor_tensor(out, a, s_, b, op0, op1), c)

            def view(b, n, w=P):
                return ps[:, b, 0:n * w].rearrange("p (n s) -> p n s", n=n)

            def mean_for_root(a, n):
                ts(a, a, 1.0 / n, EPS, ALU.mult, ALU.add, c=gave_act)

            def root_inverted(a):
                dve.wait_ge(*from_act.more())
                link(v.reciprocal(a, a))

            def inverse_root(a, n):
                mean_for_root(a, n)
                root_inverted(a)

            def square_sums(out, src, sq, n, w):
                tt(sq, src, src, ALU.mult)
                link(v.tensor_reduce(out, sq.rearrange("p (n w) -> p n w", n=n), X, ALU.add))

            def norm_T(tag, scale, shift, between=None):
                for t in range(T):
                    dve.wait_ge(*from_act.more())
                inverse_root(ssx, D)
                for t in range(T):
                    ts(RB[:, t, 0:D], x[:, t, :], ssx[:, t:t + 1], None, ALU.mult, c=gave_pe)
                if between:
                    between()
                for t in range(T):
                    for g in range(2):
                        b = bank_of(dve, (tag, t, g))
                        for i in range(4):
                            k = 4 * g + i
                            o, src = hT[:, k, t * P:(t + 1) * P], ps[:, b, i * P:(i + 1) * P]
                            c = took if i == 3 else step
                            if shift is None:
                                ts(o, src, scale[:, k:k + 1], None, ALU.mult, c=c)
                            else:
                                ts(o, src, scale[:, k:k + 1], shift[:, k:k + 1], ALU.mult, ALU.add, c=c)

            def constants():
                lamr = row("lam").rearrange("p (l i d) -> p l i d", l=DEPTH, i=4)
                for l in range(DEPTH):
                    for i in range(2):
                        c = gave_act if l == DEPTH - 1 and i == 1 else step
                        link(v.scalar_tensor_tensor(junk[:, 0:AK], lamr[:, l, 2 * i, :], 1.0, lamr[:, l, 2 * i + 1, :],
                                                    ALU.mult, ALU.mult, accum_out=small[:, 2 * l + i:2 * l + i + 1]), c)
                dve.wait_ge(*from_act.more())
                for l in range(DEPTH):
                    lam_init = 0.8 - 0.6 * math.exp(-0.3 * l)
                    tt(lamt[:, 4 + l:5 + l], lamt[:, 2 * l + 1:2 * l + 2], lamt[:, 2 * l:2 * l + 1], ALU.subtract)
                    ts(lamt[:, 4 + l:5 + l], lamt[:, 4 + l:5 + l], -lam_init, None, ALU.add)
                d, m0 = lbc[:, 3, :], lbc[:, 5, :]
                tt(d, col("lb", HEADS, HEADS), col("lb", 0, HEADS), ALU.subtract, c=gave_act)
                dve.wait_ge(*from_act.more())
                ts(m0, d, 0.0, None, ALU.min)
                tt(lbc[:, 0, :], m0, lbc[:, 4, :], ALU.subtract)
                tt(lbc[:, 1, :], lbc[:, 0, :], d, ALU.subtract)
                for g, r in enumerate(DILATIONS):
                    link(v.tensor_scalar(idx2[:, :], idx[:, :], r - 1, None, ALU.bitwise_and))
                    ts(dmask[:, g, :], idx2[:, :], 0.0, NEG, ALU.is_gt, ALU.mult)
                    tt(dmask[:, g, :], dmask[:, g, :], causal[:, :], ALU.add)
                tt(dmask[:, 0, 0:P], dmask[:, 0, 0:P], causalT[:, :], ALU.add)
                link(v.memset(qc66[:, :], 1.0))
                ts(qc66[0:64, 0:1], col("foxq")[0:64, :], 0.125, None, ALU.mult)
                link(v.tensor_copy(qc66[0:64, 1:2], col("foxk")[0:64, :]))
                inv = (np.float32(500000.0) ** (-np.arange(0, 16, 2, dtype=np.float32) / np.float32(16)))
                posf, turns_ = small[:, 16:18], cosr[:, :, :]
                link(v.tensor_copy(posf, posi[:, :]))
                for j in range(ROT):
                    ts(sinr[:, :, j:j + 1], posf.unsqueeze(2), float(inv[j]), None, ALU.mult)
                two_pi = 2 * math.pi
                c1 = 6.28125
                c2 = float(np.float32(int((two_pi - c1) * 2 ** 20) / 2 ** 20))
                c3 = two_pi - c1 - c2
                ts(turns_, sinr[:, :, :], 1 / two_pi, None, ALU.mult)
                ts(turns_, turns_, 12582912.0, None, ALU.add)
                ts(turns_, turns_, -12582912.0, None, ALU.add)
                for c_ in (c1, c2, c3):
                    stt(sinr[:, :, :], turns_, -c_, sinr[:, :, :], ALU.mult, ALU.add)
                ts(cosr[:, :, :], sinr[:, :, :], math.pi / 2, None, ALU.add)
                w = small[:, 20:36].rearrange("p (t j) -> p t j", t=T)
                ts(w, cosr[:, :, :], math.pi, -two_pi, ALU.is_gt, ALU.mult)
                tt(cosr[:, :, :], cosr[:, :, :], w, ALU.add)
                ts(cosr[:, :, :], cosr[:, :, :], 3.1415925, -3.1415925, ALU.min, ALU.max)
                ts(sinr[:, :, :], sinr[:, :, :], 3.1415925, -3.1415925, ALU.min, ALU.max, c=gave_act)
                dve.wait_ge(*from_act.more())

            def mod(l, units):
                for j in units:
                    b = bank_of(dve, ("mod", l, j))
                    part = j // 4
                    if part in (2, 5):
                        if j == 8:
                            dve.wait_ge(bgate_in, 16 * (l + 1))
                        o = gates_row[:, part // 3, (j % 4) * UC:(j % 4 + 1) * UC]
                        tt(o, ps[:, b, 0:UC], o, ALU.add, c=took)
                    else:
                        for i in range(2):
                            k = 2 * j + i
                            link(v.scalar_tensor_tensor(junk[:, :], ps[:, b, i * P:(i + 1) * P], 1.0, ident[:, :],
                                                        ALU.mult, ALU.mult, accum_out=modc[:, k:k + 1]),
                                 took if i else step)

            def mod_bias(l, lo, A, norm):
                tt(modc[:, lo:lo + 16], modc[:, lo:lo + 16], col("bmod", l * 48 + lo, 16), ALU.add)
                stt(A[:, :], modc[:, lo + 8:lo + 16], 1.0, col(norm, l * KC, KC), ALU.add, ALU.mult)

            def head_norm(Y, sq, gate=None):
                for t in range(T):
                    square_sums(meansq[:, 4 * t:4 * t + 4], Y[:, t, :, :].rearrange("p h d -> p (h d)"),
                                sq[:, 0:512], HEADS, HD)
                inverse_root(meansq[:, 0:8], HD)
                for t in range(T):
                    r = meansq[:, 4 * t:4 * t + 4].unsqueeze(2).broadcast_to([P, HEADS, HD])
                    tt(Y[:, t, :, :], Y[:, t, :, :], r, ALU.mult, c=step if gate else gave_pe)
                    if gate:
                        y = Y[:, t, :, :].rearrange("p h d -> p (h d)")
                        tt(y, y, gate(t), ALU.mult, c=gave_pe)

            def y_T(l, br, w, factor=1.0):
                for t in range(T):
                    b = bank_of(dve, ("yT", l, br, t))
                    ts(YT[:, br, :, t * P:(t + 1) * P], view(b, 4), w, factor, ALU.mult, ALU.mult, c=took)

            def diff_attention(l):
                lam_init = 0.8 - 0.6 * math.exp(-0.3 * l)
                taken(("a", l, 5))
                for t in range(T):
                    square_sums(meansq[:, 16 * t:16 * t + 16], RA[:, t, 0:1024], A_SQ, 16, AK)
                inverse_root(meansq[:, 0:32], AK)
                for t in range(T):
                    r = RA[:, t, 0:1024].rearrange("p (n d) -> p n d", n=16)
                    tt(r, r, meansq[:, 16 * t:16 * t + 16].unsqueeze(2).broadcast_to([P, 16, AK]), ALU.mult,
                       c=gave_pe)
                for t in range(T):
                    for g in range(2):
                        b = bank_of(dve, ("aT", l, t, g))
                        ts(A_QT[:, 4 * g:4 * g + 4, t * P:(t + 1) * P], view(b, 4),
                           col(("aq", "ak")[g], l), (AK ** -0.5, 1.0)[g], ALU.mult, ALU.mult, c=took)
                for t in range(T):
                    nk = (t + 1) * P
                    for h in range(HEADS):
                        b = bank_of(dve, ("aS", l, t, h))
                        d = dist[:, S - nk:S].unsqueeze(1).broadcast_to([P, 2, nk])
                        sc = A_S[:, 0:2 * nk].rearrange("p (m k) -> p m k", m=2)
                        stt(sc, d, -SLOPES[h], view(b, 2, nk), ALU.mult, ALU.add, c=took)
                        link(v.tensor_reduce(negS[:, 0:2], sc, X, ALU.max, negate=True), gave_act)
                        dve.wait_ge(*from_act.more())
                        link(v.reciprocal(recS[:, 0:2], sumS[:, 0:2]))
                        tt(recS[:, 1:2], recS[:, 1:2], lamt[:, 4 + l:5 + l], ALU.mult)
                        a = A_W[:, h % 2, 0:nk]
                        ts(a, A_E[:, 0:nk], recS[:, 0:1], None, ALU.mult)
                        stt(a, A_E[:, nk:2 * nk], recS[:, 1:2], a, ALU.mult, ALU.add, c=gave_pe)
                        n = 8 + 2 * (HEADS * t + h)
                        mod(l, range(n, n + 2))
                    b = bank_of(dve, ("aO", l, t))
                    link(v.tensor_copy(Y_A[:, t, :, :], view(b, HEADS)), took)
                head_norm(Y_A, A_SQ)
                mod_bias(l, 24, A2, "n2")
                y_T(l, 0, col("subln", l), 1.0 - lam_init)

            def hgrn(l):
                dve.wait_ge(*from_act.more())
                stt(B_E, B_B, 0.0, B_E, ALU.min, ALU.subtract)
                if l > 0:
                    for h in range(HEADS):
                        ts(B_QP[:, h, :], B_E[:, h, :], lbc[:, 3, h:h + 1], None, ALU.subtract)
                        ts(B_KP[:, h, :], B_E[:, h, :], lbc[:, 1, h:h + 1], lbc[:, 0, h:h + 1], ALU.add, ALU.max,
                           c=gave_act if h == HEADS - 1 else step)
                    for h in range(HEADS):
                        ts(B_K[:, h, :], B_K[:, h, :], lbc[:, 2, h:h + 1], None, ALU.mult)
                    dve.wait_ge(*from_act.more())
                    tt(B_E, B_KP, B_QP, ALU.add)
                for h in range(HEADS):
                    for t in range(T):
                        o, s_ = B_B[:, h, t * P:(t + 1) * P], B_E[:, h, t * P:(t + 1) * P]
                        link(v.tensor_tensor_scan(o, ones[:, :], s_, 0.0, ALU.mult, ALU.add),
                             gave_pe if h == HEADS - 1 and t else step)
                flat = lambda a: a.rearrange("p h s -> p (h s)")

                def to_middle(m):
                    n = HEADS * S // (2 * m)
                    bb = flat(B_B).rearrange("p (n w) -> p n w", n=n)
                    e = flat(B_E).rearrange("p (n w) -> p n w", n=n)
                    tt(e, bb, bb[:, :, m - 1:m].broadcast_to([P, n, 2 * m]), ALU.subtract, c=gave_act)

                to_middle(LEVELS[0])
                for t in range(T):
                    b = bank_of(dve, ("lev", l, 0, t))
                    tt(B_ATT[:, t, :, :], view(b, 4), ident[:, :].unsqueeze(1).broadcast_to([P, 4, P]), ALU.mult,
                       c=took)
                for i, m in enumerate(LEVELS):
                    dve.wait_ge(*from_act.more())
                    tt(B_QP, B_Q, B_E, ALU.mult)
                    tt(B_KP, B_K, B_E, ALU.mult, c=gave_pe)
                    if i + 1 < len(LEVELS):
                        to_middle(LEVELS[i + 1])
                    for t in range(T):
                        b = bank_of(dve, ("lev", l, i + 1, t))
                        tmp = B_TMP.rearrange("p (h s) -> p h s", h=HEADS)
                        tt(tmp, view(b, 4), lev[:, i, :].unsqueeze(1).broadcast_to([P, 4, P]), ALU.mult, c=took)
                        tt(B_ATT[:, t, :, :], B_ATT[:, t, :, :], tmp, ALU.add,
                           c=gave_act if i == len(LEVELS) - 1 and t else step)
                dve.wait_ge(*from_act.more())
                tt(B_QP[:, :, P:S], B_Q[:, :, P:S], B_E[:, :, P:S], ALU.mult)
                tt(B_KP[:, :, 0:P], B_K[:, :, 0:P], B_E[:, :, 0:P], ALU.mult, c=gave_pe)
                b = bank_of(dve, ("levx", l))
                link(v.tensor_copy(B_ATTX, view(b, 4)), took)
                for t in range(T):
                    b = bank_of(dve, ("bO", l, t))
                    link(v.tensor_copy(Y_B[:, t, :, :], view(b, HEADS)), took)
                head_norm(Y_B, B_TMP, lambda t: RB[:, t, 1536:2048])
                y_T(l, 1, col("gnorm", l))

            def mlstm(l):
                link(v.memset(C_PAD[:, :, 0:3], 0.0))
                link(v.memset(RA[:, :, 1024:1024 + HEADS * CV].rearrange("p t (h c) -> p t h c", h=HEADS)
                              [:, :, :, HD:CV], 1.0))
                b = bank_of(dve, ("cG", l))
                ts(C_I4, ps[0:4, b, 0:S], col("ib", l)[0:4, :], None, ALU.add)
                ts(C_F4, ps[0:4, b, S:2 * S], col("fb", l)[0:4, :], None, ALU.add, c=took)
                dve.wait_ge(*from_act.more())
                stt(C_B4, C_F4, 0.0, C_B4, ALU.min, ALU.subtract)
                link(v.tensor_tensor_scan(C_F4[:, 0:P], ones[0:4, :], C_B4[:, 0:P], 0.0, ALU.mult, ALU.add))
                link(v.tensor_tensor_scan(C_F4[:, P:S], ones[0:4, :], C_B4[:, P:S], C_F4[:, P - 1:P],
                                          ALU.mult, ALU.add))
                tt(C_R4, C_I4, C_F4, ALU.subtract)
                link(v.tensor_tensor_scan(C_M4, C_R4, C_R4, 0.0, ALU.max, ALU.max))
                tt(C_EM4, C_F4, C_M4, ALU.add, c=gave_act)
                taken(("cT", l, 1, 1))
                for k in range(8):
                    w = lambda j: col("convw", l * 32 + k * 4 + j)
                    ts(C_QK[:, k, :], C_PAD[:, k, 0:S], w(0), col("convb", l * 8 + k), ALU.mult, ALU.add)
                    for j in range(1, 4):
                        stt(C_QK[:, k, :], C_PAD[:, k, j:j + S], w(j), C_QK[:, k, :], ALU.mult, ALU.add,
                            c=gave_act if k == 7 and j == 3 else step)
                b = bank_of(dve, ("cR", l))
                link(v.tensor_copy(small[:, 256:272], ps[:, b, 0:16]), took)
                for hp in range(2):
                    b = bank_of(dve, ("cM", l, hp))
                    link(v.tensor_copy(C_M[:, 2 * hp:2 * hp + 2, :], view(b, 2, S)), took)
                for h in range(HEADS):
                    stt(C_G[:, 0:P], C_M[:, h, 0:P], -1.0, causalT[:, :], ALU.mult, ALU.add)
                    ts(C_G[:, P:S], C_M[:, h, P:S], -1.0, None, ALU.mult)
                    stt(C_G[:, S:S + P], C_M[:, h, P:S], -1.0, causalT[:, :], ALU.mult, ALU.add, c=gave_act)
                    dve.wait_ge(*from_act.more())
                    b = bank_of(dve, ("cw", l, h))
                    stt(C_W, ps[:, b, 0:384], HD ** -0.5, C_E, ALU.mult, ALU.mult, c=took)
                    b = bank_of(dve, ("cO", l, h))
                    o = ps[:, b, :].rearrange("p (t c) -> p t c", t=T)
                    den = small[:, 272:274]
                    em = small[:, 264:272].rearrange("p (t h) -> p t h", t=T)
                    ts(den.unsqueeze(2), o[:, :, HD:CV], -1.0, None, ALU.mult)
                    tt(den.unsqueeze(2), den.unsqueeze(2), o[:, :, HD:CV], ALU.max)
                    tt(den.unsqueeze(2), den.unsqueeze(2), em[:, :, h:h + 1], ALU.max)
                    link(v.reciprocal(den, den))
                    for t in range(T):
                        ts(Y_C[:, t, h, :], o[:, t, 0:HD], den[:, t:t + 1], None, ALU.mult,
                           c=took if t else step)
                head_norm(Y_C, C_QK.rearrange("p b s -> p (b s)"), lambda t: RA[:, t, 1540:2052])

            def merge(l, br):
                tmp = W[:, 0:1024].rearrange("p (t c) -> p t c", t=T)
                if br in (0, 2):
                    dve.wait_ge(*from_act.more())
                for j in range(2):
                    b = bank_of(dve, ("branch", l, br, j))
                    o = (br % 2) * D + j * 512
                    out = RA[:, :, j * 512:(j + 1) * 512]
                    dst = out if br == 0 else tmp
                    tt(dst, ps[:, b:b + 2, :], RB[:, :, o:o + 512], ALU.mult, c=took)
                    if br == 0:
                        continue
                    if br == 2 and j == 1:
                        for t in range(T):
                            tt(out[:, t, :], out[:, t, :], tmp[:, t, :], ALU.add, c=gave_pe)
                    else:
                        tt(out, out, tmp, ALU.add)

            def add_rows(tag, gate=None):
                tmp = RB[:, :, 2048:2304]
                for j in range(4):
                    b = bank_of(dve, (tag, j))
                    if gate is None:
                        link(v.tensor_copy(tmp, view(b, T, UC)), took)
                    else:
                        g = gate[:, j * UC:(j + 1) * UC].unsqueeze(1).broadcast_to([P, T, UC])
                        tt(tmp, view(b, T, UC), g, ALU.mult, c=took)
                    o = x[:, :, j * UC:(j + 1) * UC]
                    tt(o, o, tmp, ALU.add, c=gave_act if j == 3 else step)

            def mixer(l):
                if l == 0:
                    dve.wait_ge(inputs_in, 16 * 5)
                    dve.wait_ge(*from_act.more())
                link(v.tensor_copy(COND, cond[:, :].unsqueeze(2).broadcast_to([P, KC, P])), gave_pe)

                def first_mod():
                    if l == 0:
                        dve.wait_ge(masks_made, 1)
                    mod(l, range(8))
                    mod_bias(l, 0, A1, "n1")

                norm_T(f"n1{l}", A1, modc[:, 0:8], first_mod)
                if l == 0:
                    constants()
                diff_attention(l)
                hgrn(l)
                mlstm(l)
                merge(l, 0)
                y_T(l, 2, col("cnorm", l))
                merge(l, 1)
                merge(l, 2)
                v.memset(junk[:, 0:1], 0.0).then_inc(work_free, 1)
                add_rows(f"m{l}o", gates_row[:, 0, :])

            def hidden(l, turn=None):
                tiles = T if turn is None else 1
                for g in range(FG):
                    taken(("w1", l, g), turn)
                    b = bank_of(dve, ("w3", l, g), turn)
                    tt(hid[:, g % 2, 0:tiles, :], view(b, tiles, UC),
                       gate_h[:, g % 2, 0:tiles * UC].rearrange("p (t c) -> p t c", t=tiles), ALU.mult, c=took)
                    if turn is not None and g == FG - 3:
                        picks(1)

            def picks(e):
                for t in range(T):
                    ts(pick[:, t, :], iotaf[:, :], pos9[:, t, e:e + 1], None, ALU.is_equal,
                       c=gave_pe if t else step)

            def picked(l, name, turn=None):
                for g in range(2):
                    b = bank_of(dve, (name, l, g), turn)
                    for i in range(4):
                        k = 4 * g + i
                        ts(hT[:, k, 0:P], ps[:, b, i * P:(i + 1) * P], A2[:, k:k + 1], modc[:, 24 + k:25 + k],
                           ALU.mult, ALU.add, c=took if i == 3 else step)

            def experts(l):
                ts(pos9[:, :, 0:NE], pos_all, -float(P * (l - 1)), None, ALU.add)
                link(v.memset(pos9[:, :, NE:NE + 1], -1.0))
                link(v.tensor_copy(w9[:, :, 0:NE], w_all))
                link(v.memset(w9[:, :, NE:NE + 1], 0.0))
                picks(0)
                picked(l, "pick0")
                with turns(dve, NE, {c: gain[c.sem] for c in (took, step, gave_pe)}) as i:
                    for t in range(T):
                        ts(pick_w[:, t, :], iotaf[:, :], pos9[:, t, 0:1], w9[:, t, 0:1], ALU.is_equal, ALU.mult,
                           c=gave_pe if t else step)
                    hidden(l, i)
                    picked(l, "pick", i)
                    for a in (pos9, w9):
                        nxt = route(400, NE)
                        link(v.tensor_copy(nxt, a[:, :, 1:NE + 1]))
                        link(v.tensor_copy(a[:, :, 0:NE], nxt))
                    bank_of(dve, ("y", l), i)
                    link(v.tensor_copy(slot_rows, ps[:, 4:6, :].rearrange("p a b -> p (a b)")), took)
                    for t in range(T):
                        b = bank_of(dve, ("back", l, t), i)
                        tt(moe_sum[:, t, :], ps[:, b:b + 2, :].rearrange("p a b -> p (a b)"), moe_sum[:, t, :],
                           ALU.add, c=took)

            def ffn(l):
                norm_T(f"n2{l}", A2, modc[:, 24:32])
                if l == 0:
                    hidden(l)
                    bank_of(dve, ("y", l))
                    for t in range(T):
                        y = ps[:, 4 + 2 * t:6 + 2 * t, :].rearrange("p a b -> p (a b)")
                        tt(RB[:, t, 0:D], y, gates_row[:, 1, :], ALU.mult, c=took)
                        if t == T - 1:
                            v.memset(junk[:, 0:1], 0.0).then_inc(gates_free, 1)
                        tt(x[:, t, :], x[:, t, :], RB[:, t, 0:D], ALU.add, c=gave_act if t else step)
                    return
                b = bank_of(dve, "router")
                lg = ps[:, b, 0:T * NE].rearrange("p (t e) -> p t e", t=T)
                tt(comb[:, :, :], lg, row("rb").unsqueeze(1).broadcast_to([P, T, NE]), ALU.add, c=took)
                mx = small[:, 216:218]
                link(v.tensor_reduce(mx, comb[:, :, :], X, ALU.max))
                tt(comb[:, :, :], comb[:, :, :], mx.unsqueeze(2).broadcast_to([P, T, NE]), ALU.subtract, c=gave_act)
                cnt = small[:, 220:236].rearrange("p (t e) -> p t e", t=T)
                link(v.memset(cnt, 0.0))
                link(v.memset(moe_sum, 0.0))
                dve.wait_ge(*from_act.more())
                for t in range(T):
                    for e in range(NE):
                        me = comb[:, t, e:e + 1]
                        stt(cnt[:, t, :], comb[:, t, :], me, cnt[:, t, :], ALU.is_lt, ALU.add)
                        if e + 1 < NE:
                            stt(cnt[:, t, e + 1:NE], comb[:, t, e + 1:NE], me, cnt[:, t, e + 1:NE],
                                ALU.is_equal, ALU.add)
                ts(chosen, cnt, 2.0, None, ALU.is_lt, c=gave_pe)
                tt(w_all, chosen, comb[:, :, :], ALU.mult)
                link(v.tensor_reduce(mx, w_all, X, ALU.add))
                link(v.reciprocal(mx, mx))
                tt(w_all, w_all, mx.unsqueeze(2).broadcast_to([P, T, NE]), ALU.mult)
                b = bank_of(dve, "count")
                counts = small[:, 400:424]
                link(v.tensor_copy(counts, ps[:, b, 0:24]), took)
                tt(pos_all, counts[:, 0:T * NE].rearrange("p (t e) -> p t e", t=T), chosen, ALU.mult)
                ts(pos_all, pos_all, -1.0, None, ALU.add)
                link(v.tensor_reduce(mx[:, 0:1], counts[:, T * NE:], X, ALU.max))
                v.tensor_copy(most[:, :], mx[:, 0:1]).then_inc(most_known, 1)
                experts(1)
                dve.wait_ge(most_known, 1)
                more = dve.value_load(most[0:1, 0:1], min_val=0, max_val=S)
                before = {c: c.n for c in (took, step, gave_pe)}
                with dve.If(more > P):
                    experts(2)
                with dve.Else():
                    for c, n in before.items():
                        dve.sem_inc(c.sem, c.n - n)
                for t in range(T):
                    tt(RB[:, t, 0:D], moe_sum[:, t, :], gates_row[:, 1, :], ALU.mult)
                    tt(x[:, t, :], x[:, t, :], RB[:, t, 0:D], ALU.add, c=gave_act if t else step)

            def attention(groups, tag, mask, scale, qd, norm_rows, turned):
                rows, gate_at = (RA, RB)[qd % 2], 3 * groups * UC
                dve.wait_ge(*from_act.more())
                def score(n):
                    t, h = ATT[n]
                    nk = (t + 1) * P
                    b = bank_of(dve, (tag, "S", n))
                    src = psS[(b - 4) // 2][:, 0:groups * S].rearrange("p (g k) -> p g k", g=groups)[:, :, 0:nk]
                    d = D_S[n % 2][:, 0:groups, 0:nk]
                    stt(d, src, scale, mask[:, :, S - nk:S], ALU.mult, ALU.add, c=took)
                    link(v.tensor_reduce(negS[:, n:n + 1], d, mybir.AxisListType.XY, ALU.max, negate=True), gave_act)

                def result(n):
                    t, h = ATT[n]
                    b = bank_of(dve, (tag, "O", n))
                    link(v.reciprocal(recS[:, n:n + 1], sumS[:, n:n + 1]))
                    o = qd * UC + h * 64
                    ts(OG[:, t, o:o + 64], ps[:, b, 0:64], recS[:, n:n + 1], None, ALU.mult, c=took)

                score(0)
                for n in range(len(ATT)):
                    if n + 1 < len(ATT):
                        score(n + 1)
                    if n:
                        result(n - 1)
                    if n - NORM_STEP in range(T + 1) and qd + 1 < QUADS:
                        norm_rows(qd + 1, n - NORM_STEP)
                    if n == TURN_STEP and qd + 1 < QUADS:
                        turned(qd + 1)
                result(len(ATT) - 1)
                for t in range(T):
                    o = OG[:, t, qd * UC:(qd + 1) * UC]
                    tt(o, o, rows[:, t, gate_at:gate_at + UC], ALU.mult, c=gave_pe if qd == QUADS - 1 else step)

            def fox():
                norm_T("nfox", col("ng", 0, KC), None)
                b = bank_of(dve, "foxF")
                f = small[:, 32:64].rearrange("p (t h) -> p t h", t=T)
                tt(f, ps[:, b, 0:32].rearrange("p (t h) -> p t h", t=T),
                   row("foxbf").unsqueeze(1).broadcast_to([P, T, 16]), ALU.add, c=took)
                dve.wait_ge(*from_act.more())
                stt(small[:, 64:96], small[:, 32:64], 0.0, small[:, 64:96], ALU.min, ALU.subtract, c=gave_pe)
                b = bank_of(dve, "foxC")
                link(v.tensor_copy(small[:, 96:128], ps[:, b, 0:32]), took)
                c = small[:, 96:128].rearrange("p (t h) -> p t h", t=T)
                link(v.memset(F_QA[:, :, 0:4, 65:66], 1.0))
                link(v.memset(F_QA[:, :, 4:8, 64:65], 1.0))

                def norm_rows(qd, part):
                    rows = (RA, RB)[qd % 2]
                    if part == 0:
                        taken(("fox", qd, 1))
                        for t in range(T):
                            square_sums(meansq[:, 8 * t:8 * t + 8], rows[:, t, 0:512], D_SQ[:, 0:512], 8, 64)
                        mean_for_root(meansq[:, 0:16], 64)
                        return
                    if part == 1:
                        root_inverted(meansq[:, 0:16])
                    t = part - 1
                    r = meansq[:, 8 * t:8 * t + 8].unsqueeze(2).broadcast_to([P, 8, 64])
                    tt(F_QA[:, t, :, 0:64], rows[:, t, 0:512].rearrange("p (v d) -> p v d", v=8), r, ALU.mult)
                    if part < T:
                        return
                    cq = c[:, :, 4 * qd:4 * qd + 4].unsqueeze(3)
                    link(v.tensor_copy(F_QA[:, :, 0:4, 64:65], cq))
                    ts(F_QA[:, :, 4:8, 65:66], cq, -1.0, None, ALU.mult, c=gave_pe)

                def turned(qd):
                    for t in range(T):
                        for g in range(2):
                            b = bank_of(dve, ("foxT", qd, t, g))
                            ts(F_QT[qd % 2][0:66, 4 * g:4 * g + 4, t * P:(t + 1) * P],
                               ps[0:66, b, :].rearrange("p (n s) -> p n s", n=4), qc66[0:66, g:g + 1], None,
                               ALU.mult, c=took)

                for t in range(T + 1):
                    norm_rows(0, t)
                turned(0)
                for qd in range(QUADS):
                    attention(1, ("foxP", qd), causal[:, :].unsqueeze(1), 1.0, qd, norm_rows, turned)
                add_rows("fox2o")

            def dsw():
                norm_T("ndsw", col("ng", KC, KC), None)

                def norm_rows(qd, part):
                    rows = (RA, RB)[qd % 2]
                    if part == 0:
                        squares(qd)
                        return
                    if part == 1:
                        root_inverted(meansq[:, 0:48])
                    t = part - 1
                    r = rows[:, t, 0:1536].rearrange("p (n d) -> p n d", n=24)
                    tt(r, r, meansq[:, 24 * t:24 * t + 24].unsqueeze(2).broadcast_to([P, 24, 64]), ALU.mult)
                    rg = rows[:, t, 0:1536].rearrange("p (g h d) -> p g h d", g=6, h=4)
                    wg = row("dswg").rearrange("p (g d) -> p g d", g=6).unsqueeze(2).broadcast_to([P, 6, 4, 64])
                    tt(rg, rg, wg, ALU.mult)
                    a, b_ = r[:, :, 0:ROT], r[:, :, ROT:2 * ROT]
                    cc = cosr[:, t, :].unsqueeze(1).broadcast_to([P, 24, ROT])
                    ss = sinr[:, t, :].unsqueeze(1).broadcast_to([P, 24, ROT])
                    w = [D_SQ[:, i * 192:(i + 1) * 192].rearrange("p (n j) -> p n j", n=24) for i in range(4)]
                    for o, i0, i1 in ((w[0], a, cc), (w[1], b_, ss), (w[2], b_, cc), (w[3], a, ss)):
                        tt(o, i0, i1, ALU.mult)
                    tt(a, w[0], w[1], ALU.subtract)
                    tt(b_, w[2], w[3], ALU.add, c=gave_pe if t else step)

                def squares(qd):
                    rows = (RA, RB)[qd % 2]
                    taken(("dsw", qd, 5))
                    for t in range(T):
                        for i in range(2):
                            o = 24 * t + 12 * i
                            square_sums(meansq[:, o:o + 12], rows[:, t, 768 * i:768 * (i + 1)], D_SQ[:, 0:768],
                                        12, 64)
                    mean_for_root(meansq[:, 0:48], 64)

                for t in range(T + 1):
                    norm_rows(0, t)
                for qd in range(QUADS):
                    attention(DG, ("dswP", qd), dmask[:, :, :], 0.125, qd, norm_rows, lambda qd: None)
                add_rows("dsw2o")

            mixer(0)
            if want("ffn0"):
                ffn(0)
            if want("mix1"):
                mixer(1)
            if want("moe"):
                ffn(1)
            if want("fox"):
                fox()
            if want("dsw"):
                dsw()
            v.memset(junk[:, 0:1], 0.0).then_inc(out_ready, 1)


def unit_of(w, c0, n=UC):
    k = w.shape[0] // P
    return w[:, c0:c0 + n].reshape(k, P, n).transpose(1, 0, 2).reshape(P, k * n)


def columns(a):
    return np.asarray(a).reshape(-1, P).T


def lay_out(inp):
    before, experts, after = stream_plan()
    units = before + experts + after
    stream = np.empty((len(units), P, UNIT), np.float32)
    w_in, w_branch, w_out, w_mod = inp["w_in"], inp["w_branch"], inp["w_out"], inp["w_mod"]
    starts = {n: [c for lo, hi in spans for c in range(lo, hi, UC)]
              for n, spans in (("a", W_IN_A), ("b", W_IN_B), ("c", W_IN_C))}
    ffns = {"f": [inp[n] for n in ("ffn_w1", "ffn_w3", "ffn_w2")],
            "m": [inp[n][0] for n in ("moe_w1", "moe_w3", "moe_w2")]}
    for u, (name, l, j) in enumerate(units):
        if name == "mod":
            stream[u] = unit_of(w_mod[l], j * UC)
        elif name in starts:
            stream[u] = unit_of(w_in[l], starts[name][j])
        elif name == "gate":
            stream[u] = unit_of(w_in[l], W_IN_GATE + j * UC)
        elif name == "branch":
            stream[u] = unit_of(w_branch[l, j // 2], (j % 2) * 512, 512)
        elif name == "out":
            stream[u] = unit_of(w_out[l], j * UC)
        elif name[:2] in ("w1", "w3"):
            stream[u] = unit_of(ffns[name[2]][name[1] == "3"][l], j * UC)
        elif name[:2] == "w2":
            stream[u] = unit_of(ffns[name[2]][2][l][j * UC:(j + 1) * UC], 0, D)
        elif name == "fox":
            stream[u] = unit_of(inp["fox_w_in_2"][0], (j % 4) * D + (j // 4) * UC)
        elif name == "foxo":
            stream[u] = unit_of(inp["fox_w_out_2"][0], j * UC)
        elif name == "dsw":
            stream[u] = unit_of(inp["dsw_w_in_2"][0], (j % 10) * D + (j // 10) * UC)
        elif name == "dswo":
            stream[u] = unit_of(inp["dsw_w_out_2"][0], j * UC)
    cols = np.zeros((P, N_COLS), np.float32)

    def put(name, a, lo=0):
        o = COLS[name][0] + lo
        cols[0:a.shape[0], o:o + a.shape[1]] = a

    put("c", columns(inp["c"]))
    put("ng", columns(inp["norm_g_2"].reshape(-1)))
    for l in range(DEPTH):
        put("bmod", columns(inp["b_mod"][l]), l * 48)
        put("n1", columns(inp["norm1_w"][l]), l * KC)
        put("n2", columns(inp["norm2_w"][l]), l * KC)
        put("convw", inp["c_conv_w"][l].reshape(4, 8, P).transpose(2, 1, 0).reshape(P, 32), l * 32)
        put("convb", columns(inp["c_conv_b"][l]), l * 8)
        for name, key in (("aq", "a_qnorm_w"), ("ak", "a_knorm_w")):
            put(name, np.concatenate([inp[key][l]] * 2)[:, None], l)
        for name, key in (("subln", "a_subln_w"), ("gnorm", "b_gnorm_w"), ("cnorm", "c_norm_w"),
                          ("ib", "c_igate_b"), ("fb", "c_fgate_b")):
            put(name, inp[key][l][:, None], l)
        put("lb", columns(inp["b_lb_logits"][l]), l * HEADS)
        put("wif", unit_of(w_in[l], W_IN_IF, 8), l * KC * 8)
    put("router", unit_of(inp["moe_router_w"][0], 0, NE))
    put("foxwf", unit_of(inp["fox_w_in_2"][0], 4 * D, 16))
    put("foxq", inp["fox_q_norm_2"][0][:, None])
    put("foxk", inp["fox_k_norm_2"][0][:, None])
    lam = np.stack([inp[f"a_lambda_{n}"] for n in ("q1", "k1", "q2", "k2")], axis=1).reshape(-1)
    rows = np.concatenate([lam, inp["moe_router_b"].reshape(-1), inp["fox_b_f_2"].reshape(-1),
                           inp["dsw_q_norm_2"].reshape(-1), inp["dsw_k_norm_2"].reshape(-1)])[None, :]
    bgate = np.concatenate([inp["b_mod"][:, 2 * D:3 * D], inp["b_mod"][:, 5 * D:6 * D]], axis=1)
    return {"stream": stream, "cols": cols, "rows": rows, "bgate": bgate, "x": inp["x"][0],
            "pos": inp["positions_2"].reshape(T, P).T}


def kernel(**inputs):
    import concourse.bacc as bacc
    from concourse.bass_utils import run_bass_kernel_spmd

    nc = bacc.Bacc("TRN2", target_bir_lowering=False, num_devices=1)
    arrays = {k: np.ascontiguousarray(a)
              for k, a in lay_out({k: np.asarray(v) for k, v in inputs.items()}).items()}
    args = [nc.dram_tensor(k, a.shape, mybir.dt.from_np(a.dtype), kind="ExternalInput").ap()
            for k, a in arrays.items()]
    out = nc.dram_tensor("out", (S, D), F32, kind="ExternalOutput").ap()
    two_blocks(nc, *args, out)
    r = run_bass_kernel_spmd(nc, [arrays], core_ids=[0])
    return r.results[0]["out"].reshape(1, S, D)
```
